# Optimizing a Trainium2 kernel written in Bass

```python
import math
import jax, jax.numpy as jnp
from jax import lax
import numpy as np

D_MODEL = 1024
BATCH = 1
SEQ = 512
DEPTH = 2

N_A = DEPTH // 2
N_B = DEPTH - N_A
HEAD_DIM = 64
ROPE_DIM = HEAD_DIM // 4
ROPE_THETA = 500000.0
RMS_EPS = 1e-6
NEG_INF = -1e30
MEM_HEADS = 4
MEM_WIDTH = MEM_HEADS * HEAD_DIM
MIX_WIDTH = D_MODEL
LRU_WIDTH = MIX_WIDTH - MEM_WIDTH
LRU_BLOCKS = LRU_WIDTH // HEAD_DIM
CONV_WIDTH = 4
LRU_C = 8.0
NSA_WIDTH = MIX_WIDTH - MEM_WIDTH
NSA_HEADS = NSA_WIDTH // HEAD_DIM
NSA_KV_HEADS = 2
N_BRANCH = 3
CMP_LEN = 32
CMP_STRIDE = 16
CMP_HIDDEN = 256
SEL_LEN = 64
SEL_TOP = 16
SEL_FORCE_SCORE = 1e4
WINDOW = 512
Q_CHUNK = 64
N_KEYS = 128
N_EXPERTS = N_KEYS * N_KEYS
PEER_HEADS = 8
PEER_KEY_DIM = 256
PEER_TOPK = 16
PEER_CHUNK_MAX = 512

kernel_name = "hybrid_rglru_nsa_peer_yoco"

def rmsnorm(x, g):
    xf = x.astype(jnp.float32)
    y = xf * lax.rsqrt(jnp.mean(xf * xf, axis=-1, keepdims=True) + RMS_EPS)
    return (y * g.astype(jnp.float32)).astype(x.dtype)

def rope(x, pos):
    half = ROPE_DIM // 2
    freqs = ROPE_THETA ** (-jnp.arange(half, dtype=jnp.float32) / half)
    ang = pos.astype(jnp.float32)[:, None] * freqs[None, :]
    cos = jnp.cos(ang)[:, None, :]
    sin = jnp.sin(ang)[:, None, :]
    xf = x.astype(jnp.float32)
    x1, x2, rest = xf[..., :half], xf[..., half:ROPE_DIM], xf[..., ROPE_DIM:]
    out = jnp.concatenate([x1 * cos - x2 * sin, x2 * cos + x1 * sin, rest], axis=-1)
    return out.astype(x.dtype)

def masked_softmax(s, mask):
    s = jnp.where(mask, s.astype(jnp.float32), NEG_INF)
    p = jax.nn.softmax(s, axis=-1)
    return jnp.where(mask, p, 0.0)

def causal_conv(x, w, b):
    K, C = w.shape
    y = lax.conv_general_dilated(x, w[:, None, :].astype(x.dtype), window_strides=(1,),
                                 padding=[(K - 1, 0)], dimension_numbers=('NWC', 'WIO', 'NWC'),
                                 feature_group_count=C)
    return y + b.astype(x.dtype)

def rg_lru(x, gate_w, gate_b, lam):
    B, S, C = x.shape
    xb = x.reshape(B, S, LRU_BLOCKS, HEAD_DIM)
    gates = jnp.einsum('bsnd,gnde->gbsne', xb, gate_w).reshape(2, B, S, C).astype(jnp.float32)
    gates = gates + gate_b.astype(jnp.float32)[:, None, None, :]
    r = jax.nn.sigmoid(gates[0])
    i = jax.nn.sigmoid(gates[1])
    log_a = -LRU_C * r * jax.nn.softplus(-lam.astype(jnp.float32))
    a = jnp.exp(log_a)
    u = jnp.sqrt(-jnp.expm1(2.0 * log_a)) * (i * x.astype(jnp.float32))

    def combine(left, right):
        a1, b1 = left
        a2, b2 = right
        return a1 * a2, a2 * b1 + b2

    _, h = lax.associative_scan(combine, (a, u), axis=1)
    return h.astype(x.dtype)

def memory_attention(qm, mem, norm_g, w_kv, q_gain, k_gain):
    B, S, _ = qm.shape
    M = mem.shape[1]
    kv = (rmsnorm(mem, norm_g) @ w_kv).reshape(B, M, 2, MEM_HEADS, HEAD_DIM)
    q = rmsnorm(qm.reshape(B, S, MEM_HEADS, HEAD_DIM), q_gain)
    k = rmsnorm(kv[:, :, 0], k_gain)
    v = kv[:, :, 1]
    s = jnp.einsum('bshd,bmhd->bhsm', q, k) * (HEAD_DIM ** -0.5)
    p = jax.nn.softmax(s.astype(jnp.float32), axis=-1).astype(v.dtype)
    return jnp.einsum('bhsm,bmhd->bshd', p, v).reshape(B, S, MEM_WIDTH)

def nsa_shared_kv(x, positions, kv_norm, w_kv_shared, k_gain_shared, cmp_pos, cmp_w1, cmp_b1, cmp_w2):
    B, S, _ = x.shape
    G, dh = NSA_KV_HEADS, HEAD_DIM
    kv = (rmsnorm(x, kv_norm) @ w_kv_shared).reshape(B, S, N_BRANCH, 2, G, dh)
    n_cmp = (S - CMP_LEN) // CMP_STRIDE + 1
    idx = np.arange(n_cmp)[:, None] * CMP_STRIDE + np.arange(CMP_LEN)[None, :]

    def compress(tok, j):
        blk = tok[:, idx] + cmp_pos[j][None, None, :, None, :]
        blk = blk.transpose(0, 1, 3, 2, 4).reshape(B, n_cmp, G, CMP_LEN * dh)
        hid = jax.nn.gelu(blk @ cmp_w1[j] + cmp_b1[j])
        return hid @ cmp_w2[j]

    kc = rope(rmsnorm(compress(kv[:, :, 0, 0], 0), k_gain_shared[0]), positions[idx[:, -1]])
    vc = compress(kv[:, :, 0, 1], 1)
    ks = rope(rmsnorm(kv[:, :, 1, 0], k_gain_shared[1]), positions)
    vs = kv[:, :, 1, 1]
    kw = rope(rmsnorm(kv[:, :, 2, 0], k_gain_shared[2]), positions)
    vw = kv[:, :, 2, 1]
    t = lambda a: a.transpose(0, 2, 1, 3)
    return (t(kc), t(vc), t(ks), t(vs), t(kw), t(vw))

def _cmp_sel_overlap(n_cmp, n_sel):
    c0 = np.arange(n_cmp)[:, None] * CMP_STRIDE
    s0 = np.arange(n_sel)[None, :] * SEL_LEN
    ov = np.minimum(c0 + CMP_LEN, s0 + SEL_LEN) - np.maximum(c0, s0)
    return (np.clip(ov, 0, None) / CMP_LEN).astype(np.float32)

def nsa_attention(q, kc, vc, ks, vs, kw, vw):
    B, S, H, dh = q.shape
    G = kc.shape[1]
    R = H // G
    C = Q_CHUNK
    NQ = S // C
    n_cmp = kc.shape[2]
    n_sel = S // SEL_LEN
    top = min(SEL_TOP, n_sel)
    scale = dh ** -0.5
    cmp_end = jnp.arange(n_cmp) * CMP_STRIDE + CMP_LEN - 1
    overlap = jnp.asarray(_cmp_sel_overlap(n_cmp, n_sel))
    ks_blk = ks.reshape(B, G, n_sel, SEL_LEN, dh)
    vs_blk = vs.reshape(B, G, n_sel, SEL_LEN, dh)
    kw_pad = jnp.pad(kw, ((0, 0), (0, 0), (WINDOW, 0), (0, 0)))
    vw_pad = jnp.pad(vw, ((0, 0), (0, 0), (WINDOW, 0), (0, 0)))
    q_chunks = q.reshape(B, NQ, C, G, R, dh).transpose(1, 0, 3, 4, 2, 5)
    b_ix = jnp.arange(B)[:, None, None, None]
    g_ix = jnp.arange(G)[None, :, None, None]
    blk_ids = jnp.arange(n_sel)

    def chunk(args):
        qc, c = args
        t = c * C + jnp.arange(C)
        s = jnp.einsum('bgrqd,bgnd->bgrqn', qc, kc) * scale
        p_cmp = masked_softmax(s, cmp_end[None, :] <= t[:, None]).astype(vc.dtype)
        o_cmp = jnp.einsum('bgrqn,bgnd->bgrqd', p_cmp, vc)
        imp = jnp.einsum('bgrqn,nj->bgqj', p_cmp, overlap.astype(p_cmp.dtype)).astype(jnp.float32)
        cur = t // SEL_LEN
        valid = blk_ids[None, :] <= cur[:, None]
        forced = (blk_ids[None, :] == 0) | (blk_ids[None, :] == cur[:, None]) | (blk_ids[None, :] == cur[:, None] - 1)
        imp = jnp.where(forced, SEL_FORCE_SCORE, imp)
        imp = jnp.where(valid, imp, -1.0)
        vals, idx = lax.top_k(imp, top)
        kg = ks_blk[b_ix, g_ix, idx]
        vg = vs_blk[b_ix, g_ix, idx].reshape(B, G, C, top * SEL_LEN, dh)
        s = jnp.einsum('bgrqd,bgqkld->bgrqkl', qc, kg) * scale
        kpos = idx[..., None] * SEL_LEN + jnp.arange(SEL_LEN)
        m = (vals >= 0.0)[..., None] & (kpos <= t[None, None, :, None, None])
        p_sel = masked_softmax(s.reshape(B, G, R, C, top * SEL_LEN),
                               m.reshape(B, G, 1, C, top * SEL_LEN)).astype(vg.dtype)
        o_sel = jnp.einsum('bgrqk,bgqkd->bgrqd', p_sel, vg)
        kwin = lax.dynamic_slice_in_dim(kw_pad, c * C, WINDOW + C, axis=2)
        vwin = lax.dynamic_slice_in_dim(vw_pad, c * C, WINDOW + C, axis=2)
        wpos = c * C - WINDOW + jnp.arange(WINDOW + C)
        m = (wpos[None, :] <= t[:, None]) & (wpos[None, :] > t[:, None] - WINDOW) & (wpos[None, :] >= 0)
        s = jnp.einsum('bgrqd,bgkd->bgrqk', qc, kwin) * scale
        p_win = masked_softmax(s, m).astype(vwin.dtype)
        o_win = jnp.einsum('bgrqk,bgkd->bgrqd', p_win, vwin)
        return (o_cmp, o_sel, o_win)

    outs = lax.map(chunk, (q_chunks, jnp.arange(NQ)))
    back = lambda o: o.transpose(1, 0, 4, 2, 3, 5).reshape(B, S, H, dh)
    return (back(outs[0]), back(outs[1]), back(outs[2]))

def peer(h, w_q, sub_keys, u_tab, v_tab):
    B, S, D = h.shape
    T = B * S
    ch = math.gcd(T, PEER_CHUNK_MAX)
    half = PEER_KEY_DIM // 2

    def chunk(xc):
        q = (xc @ w_q).reshape(ch, PEER_HEADS, 2, half)
        s = jnp.einsum('thpd,hpnd->thpn', q, sub_keys).astype(jnp.float32)
        v1, i1 = lax.top_k(s[:, :, 0], PEER_TOPK)
        v2, i2 = lax.top_k(s[:, :, 1], PEER_TOPK)
        cand = (v1[..., :, None] + v2[..., None, :]).reshape(ch, PEER_HEADS, PEER_TOPK * PEER_TOPK)
        vals, ci = lax.top_k(cand, PEER_TOPK)
        e = (jnp.take_along_axis(i1, ci // PEER_TOPK, axis=-1) * N_KEYS
             + jnp.take_along_axis(i2, ci % PEER_TOPK, axis=-1))
        g = jax.nn.softmax(vals, axis=-1).astype(xc.dtype)
        u = u_tab[e]
        act = jax.nn.gelu(jnp.einsum('td,thkd->thk', xc, u)) * g
        return jnp.einsum('thk,thkd->td', act, v_tab[e])

    return lax.map(chunk, h.reshape(T // ch, ch, D)).reshape(B, S, D)

def setup_inputs(seed: int = 0) -> dict:
    key = jax.random.key(seed)
    counter = [0]

    def nk():
        counter[0] += 1
        return jax.random.fold_in(key, counter[0])

    def nrm(shape, scale):
        return scale * jax.random.normal(nk(), shape, jnp.float32)

    def gain(shape):
        return 1.0 + 0.02 * jax.random.normal(nk(), shape, jnp.float32)

    D = D_MODEL
    u = jax.random.uniform(nk(), (N_A, LRU_WIDTH), jnp.float32, minval=0.9, maxval=0.999)
    a0 = u ** (1.0 / LRU_C)
    a_lambda = jnp.log(a0) - jnp.log1p(-a0)
    return {
        "x": nrm((BATCH, SEQ, D), 1.0),
        "mem": nrm((BATCH, 256, D), 1.0),
        "positions": jnp.arange(SEQ, dtype=jnp.int32),
        "norm_mix": gain((DEPTH, D)),
        "norm_ffn": gain((DEPTH, D)),
        "norm_mem": gain((DEPTH, D)),
        "w_out": nrm((DEPTH, MIX_WIDTH, D), MIX_WIDTH ** -0.5),
        "w_mem_kv": nrm((DEPTH, D, 2 * MEM_WIDTH), D ** -0.5),
        "mem_q_gain": gain((DEPTH, HEAD_DIM)),
        "mem_k_gain": gain((DEPTH, HEAD_DIM)),
        "a_w_in": nrm((N_A, D, 2 * LRU_WIDTH + MEM_WIDTH), D ** -0.5),
        "a_conv_w": nrm((N_A, CONV_WIDTH, LRU_WIDTH), CONV_WIDTH ** -0.5),
        "a_conv_b": nrm((N_A, LRU_WIDTH), 0.02),
        "a_gate_w": nrm((N_A, 2, LRU_BLOCKS, HEAD_DIM, HEAD_DIM), HEAD_DIM ** -0.5),
        "a_gate_b": nrm((N_A, 2, LRU_WIDTH), 0.02),
        "a_lambda": a_lambda,
        "b_w_in": nrm((N_B, D, NSA_WIDTH + N_BRANCH * NSA_HEADS + MEM_WIDTH), D ** -0.5),
        "b_gate_b": nrm((N_B, N_BRANCH * NSA_HEADS), 0.02),
        "b_q_gain": gain((N_B, HEAD_DIM)),
        "kv_norm": gain((D,)),
        "w_kv_shared": nrm((D, N_BRANCH * 2 * NSA_KV_HEADS * HEAD_DIM), D ** -0.5),
        "k_gain_shared": gain((N_BRANCH, HEAD_DIM)),
        "cmp_pos": nrm((2, CMP_LEN, HEAD_DIM), 0.1),
        "cmp_w1": nrm((2, CMP_LEN * HEAD_DIM, CMP_HIDDEN), (CMP_LEN * HEAD_DIM) ** -0.5),
        "cmp_b1": nrm((2, CMP_HIDDEN), 0.02),
        "cmp_w2": nrm((2, CMP_HIDDEN, HEAD_DIM), CMP_HIDDEN ** -0.5),
        "peer_wq": nrm((DEPTH, D, PEER_HEADS * PEER_KEY_DIM), D ** -0.5),
        "peer_subkeys": nrm((DEPTH, PEER_HEADS, 2, N_KEYS, PEER_KEY_DIM // 2), (PEER_KEY_DIM // 2) ** -0.5),
        "peer_u": nrm((DEPTH, N_EXPERTS, D), D ** -0.5),
        "peer_v": nrm((DEPTH, N_EXPERTS, D), PEER_HEADS ** -0.5),
    }

def reference(x, mem, positions, norm_mix, norm_ffn, norm_mem, w_out, w_mem_kv, mem_q_gain, mem_k_gain,
              a_w_in, a_conv_w, a_conv_b, a_gate_w, a_gate_b, a_lambda, b_w_in, b_gate_b, b_q_gain,
              kv_norm, w_kv_shared, k_gain_shared, cmp_pos, cmp_w1, cmp_b1, cmp_w2,
              peer_wq, peer_subkeys, peer_u, peer_v):
    B, S, _ = x.shape
    shared = None
    for l in range(DEPTH):
        h = rmsnorm(x, norm_mix[l])
        if l < N_A:
            proj = h @ a_w_in[l]
            xb = causal_conv(proj[..., :LRU_WIDTH], a_conv_w[l], a_conv_b[l])
            yb = proj[..., LRU_WIDTH:2 * LRU_WIDTH]
            qm = proj[..., 2 * LRU_WIDTH:]
            mix = rg_lru(xb, a_gate_w[l], a_gate_b[l], a_lambda[l]) * jax.nn.gelu(yb)
        else:
            j = l - N_A
            proj = h @ b_w_in[j]
            q = proj[..., :NSA_WIDTH].reshape(B, S, NSA_HEADS, HEAD_DIM)
            gl = (proj[..., NSA_WIDTH:NSA_WIDTH + N_BRANCH * NSA_HEADS].reshape(B, S, NSA_HEADS, N_BRANCH)
                  + b_gate_b[j].reshape(NSA_HEADS, N_BRANCH))
            qm = proj[..., NSA_WIDTH + N_BRANCH * NSA_HEADS:]
            q = rope(rmsnorm(q, b_q_gain[j]), positions)
            o_cmp, o_sel, o_win = nsa_attention(q, shared[0], shared[1], shared[2], shared[3], shared[4], shared[5])
            g = jax.nn.sigmoid(gl.astype(jnp.float32)).astype(q.dtype)
            mix = (g[..., 0:1] * o_cmp + g[..., 1:2] * o_sel + g[..., 2:3] * o_win).reshape(B, S, NSA_WIDTH)
        mo = memory_attention(qm, mem, norm_mem[l], w_mem_kv[l], mem_q_gain[l], mem_k_gain[l])
        x = x + jnp.concatenate([mix, mo], axis=-1) @ w_out[l]
        x = x + peer(rmsnorm(x, norm_ffn[l]), peer_wq[l], peer_subkeys[l], peer_u[l], peer_v[l])
        if l == N_A - 1:
            shared = nsa_shared_kv(x, positions, kv_norm, w_kv_shared, k_gain_shared,
                                   cmp_pos, cmp_w1, cmp_b1, cmp_w2)
    return x


_drawn_inputs = setup_inputs


def setup_inputs(seed=0):
    import zlib

    import numpy as np

    out = dict(_drawn_inputs(seed))
    spreads = {}
    factors = {'norm_mem': 3.827,
     'mem_q_gain': 4.147,
     'mem_k_gain': 4.356,
     'a_gate_b': 3.178,
     'b_gate_b': 8.0,
     'b_q_gain': 6.467,
     'kv_norm': 4.955,
     'k_gain_shared': 6.18,
     'cmp_b1': 4.496}
    for name, (base, spread) in spreads.items():
        noise = np.random.default_rng([zlib.crc32(name.encode()), seed]).standard_normal(out[name].shape)
        drawn = base * np.exp(spread * noise) if base else spread * noise
        out[name] = __import__('jax').numpy.asarray(drawn.astype(out[name].dtype))
    for name, factor in factors.items():
        out[name] = (out[name] * factor).astype(out[name].dtype)
    return out
```

```python
from contextlib import ExitStack

import numpy as np

import concourse.bass as bass
from concourse import mybir

F32 = mybir.dt.float32
F32R = mybir.dt.float32r
I32 = mybir.dt.int32
U32 = mybir.dt.uint32
ALU = mybir.AluOpType
ACT = mybir.ActivationFunctionType
AX = mybir.AxisListType

P = 128
D = 1024
S = 512
DC = D // P
TT = S // P
HD = 64
EPS = 1e-6
NEG = -1e30
LRU_CH = 6
MEM_CH = 2
MEMLEN = 256
MT = MEMLEN // P
LAYERS = 2
ROPE_HALF = 8
THETA = 500000.0
N_CMP = 31
CMPW = 32
CMP_STRIDE = 16
CMP_LEN = 32
HID = 256
SCALE = HD ** -0.5
PH = 8
TOPK = 16
HK = PH * TOPK
NK = 128
TB = 64
NTB = S // TB
GT = 2
NG = NK // GT

COLS = [
    ("norm_mix0", 8), ("norm_mix1", 8), ("norm_ffn0", 8), ("norm_ffn1", 8), ("norm_mem0", 8), ("norm_mem1", 8),
    ("kv_norm", 8), ("conv_w", 4 * LRU_CH), ("conv_b", LRU_CH), ("gate_b", 2 * LRU_CH), ("lam", LRU_CH),
    ("mq_gain0", 1), ("mq_gain1", 1), ("mk_gain0", 1), ("mk_gain1", 1), ("q_gain", 1), ("k_gain", 3),
    ("cmp_b1", 4), ("nsa_gate_b", 36), ("cmp_pos", 32),
    ("freq", 1), ("rowvalid", 1), ("ident", P), ("rot", P), ("headmean", P), ("causal", P), ("cmpmask", TT * CMPW),
    ("iota", P),
]
OFF = {}
_at = 0
for _n, _w in COLS:
    OFF[_n] = (_at, _w)
    _at += _w
NCOLS = _at


class Signal:

    def __init__(self, sem, credit=0):
        self.sem, self.base, self.credit = sem, 0, credit
        self.given = False

    def free(self, n):
        return self.base + n + 1

    def done(self, n):
        return self.base + self.credit + n + 1

    def passed(self, n):
        self.base += n

    def give(self, eng):
        if not self.given:
            self.given = True
            eng.sem_inc(self.sem, self.credit)


class Chip:

    def __init__(self, nc, ctx):
        self.nc, self.ctx, self.signals = nc, ctx, {}

    def sb(self, ctx, name, shape, dt=F32):
        return ctx.enter_context(self.nc.sbuf_tensor(name, shape, dt))

    def ps(self, ctx, name, shape, dt=F32):
        return ctx.enter_context(self.nc.psum_tensor(name, shape, dt))

    def sig(self, name, credit=0):
        if name not in self.signals:
            self.signals[name] = Signal(self.ctx.enter_context(self.nc.semaphore(name)), credit)
        return self.signals[name]

    def col(self, name, a=0, n=None):
        at, w = OFF[name]
        n = w - a if n is None else n
        return self.params[:, at + a:at + a + n]


def bc(ap, shape):
    return ap.to_broadcast(shape)


def load(k, name, pairs):
    nc = k.nc
    loaded = k.sig("loaded")
    with nc.Block() as block:
        @block.sync
        def _(sp):
            for dst, src in pairs:
                sp.dma_start(dst, src).then_inc(loaded.sem, 16)
            sp.wait_ge(loaded.sem, loaded.base + 16 * len(pairs))
    loaded.passed(16 * len(pairs))


def norm_transpose(k, name, src, nt, gain, out):
    nc = k.nc
    squares, mean_ready, std_ready = k.sig("nt_squares"), k.sig("nt_mean"), k.sig("nt_std")
    scaled, turned, stored = k.sig("nt_scaled"), k.sig("nt_turned"), k.sig("nt_stored", 4)
    with ExitStack() as c:
        xn = k.sb(c, name + "_xn", [P, nt, D])
        dump = k.sb(c, name + "_dump", [P, D])
        ssq = k.sb(c, name + "_ssq", [P, nt])
        std = k.sb(c, name + "_std", [P, nt])
        rstd = k.sb(c, name + "_rstd", [P, nt])
        ps = k.ps(c, name + "_ps", [P, 4, 4, P])
        block = c.enter_context(nc.Block())
        ident = k.col("ident")

        @block.scalar
        def _(act):
            for t in range(nt):
                act.activation(dump[:], src[:, t, :], ACT.Square, accum_out=ssq[:, t:t + 1]).then_inc(squares.sem, 1)
                act.drain()
            act.wait_ge(mean_ready.sem, mean_ready.done(0))
            act.activation(std[:], ssq[:], ACT.Sqrt).then_inc(std_ready.sem, 1)

        @block.vector
        def _(dve):
            stored.give(dve)
            dve.wait_ge(squares.sem, squares.done(nt - 1))
            dve.tensor_scalar(ssq[:], ssq[:], 1.0 / D, EPS, ALU.mult, ALU.add).then_inc(mean_ready.sem, 1)
            dve.wait_ge(std_ready.sem, std_ready.done(0))
            dve.reciprocal(rstd[:], std[:])
            dve.drain()
            for t in range(nt):
                dve.tensor_scalar(xn[:, t, :], src[:, t, :], rstd[:, t:t + 1], None, ALU.mult).then_inc(scaled.sem, 1)
            for n in range(2 * nt):
                t, h = n // 2, n % 2
                dve.wait_ge(turned.sem, turned.done(n))
                dve.tensor_tensor(out[:, 4 * h:4 * h + 4, t * P:(t + 1) * P], ps[:, n % 4, :, :],
                                  bc(gain[:, 4 * h:4 * h + 4].unsqueeze(2), [P, 4, P]), ALU.mult).then_inc(stored.sem, 1)

        @block.tensor
        def _(pe):
            for n in range(2 * nt):
                t, h = n // 2, n % 2
                pe.wait_ge(scaled.sem, scaled.done(t))
                pe.wait_ge(stored.sem, stored.free(n))
                for q in range(4):
                    ch = 4 * h + q
                    last = pe.transpose(ps[:, n % 4, q, :], xn[:, t, ch * P:(ch + 1) * P], ident)
                last.then_inc(turned.sem, 1)
    squares.passed(nt)
    mean_ready.passed(1)
    std_ready.passed(1)
    scaled.passed(nt)
    turned.passed(2 * nt)
    stored.passed(2 * nt)


def project(k, name, w, n, rhs, width, out):
    nc = k.nc
    loaded = [k.sig("pj_loaded0"), k.sig("pj_loaded1")]
    product, stored = k.sig("pj_product", 2), k.sig("pj_stored", 2)
    rounds = n // 2
    with ExitStack() as c:
        wb = k.sb(c, name + "_w", [P, 2, DC, P])
        ps = k.ps(c, name + "_ps", [P, 2, 512])
        block = c.enter_context(nc.Block())

        @block.sync
        def _(sp):
            with sp.Fori(0, rounds) as r:
                for b in range(2):
                    sp.wait_ge(product.sem, r * 2 + product.free(b))
                    sp.dma_start(wb[:, b, :, :], w[bass.ds(r * 2 + b, 1), :, :, :].rearrange("a p c m -> p (a c) m")
                                 ).then_inc(loaded[b].sem, 16)

        @block.tensor
        def _(pe):
            product.give(pe)
            with pe.Fori(0, rounds) as r:
                for b in range(2):
                    pe.wait_ge(loaded[b].sem, r * 16 + loaded[b].base + 16)
                    pe.wait_ge(stored.sem, r * 2 + stored.free(b))
                    for dc in range(DC):
                        last = pe.matmul(ps[:, b, 0:width], wb[:, b, dc, :], rhs[:, dc, :],
                                         start=(dc == 0), stop=(dc == DC - 1))
                    last.then_inc(product.sem, 1)

        @block.scalar
        def _(act):
            stored.give(act)
            with act.Fori(0, rounds) as r:
                for b in range(2):
                    act.wait_ge(product.sem, r * 2 + product.done(b))
                    act.activation(out[:, bass.ds(r * 2 + b, 1), :].rearrange("p a n -> p (a n)"), ps[:, b, 0:width],
                                   ACT.Copy).then_inc(stored.sem, 1)
    for s in loaded:
        s.passed(16 * rounds)
    product.passed(n)
    stored.passed(n)


def natural(k, name, w, width, lhs, nt, out):
    nc = k.nc
    loaded, product = k.sig("na_loaded"), k.sig("na_product")
    with ExitStack() as c:
        wb = k.sb(c, name + "_w", [P, DC, width])
        ps = k.ps(c, name + "_ps", [P, nt, 512])
        block = c.enter_context(nc.Block())

        @block.sync
        def _(sp):
            sp.dma_start(wb[:], w).then_inc(loaded.sem, 16)

        @block.tensor
        def _(pe):
            pe.wait_ge(loaded.sem, loaded.base + 16)
            for t in range(nt):
                for dc in range(DC):
                    last = pe.matmul(ps[:, t, 0:width], lhs[:, dc, t * P:(t + 1) * P], wb[:, dc, :],
                                     start=(dc == 0), stop=(dc == DC - 1))
                last.then_inc(product.sem, 1)

        @block.scalar
        def _(act):
            for t in range(nt):
                act.wait_ge(product.sem, product.done(t))
                act.activation(out[:, t, :], ps[:, t, 0:width], ACT.Copy)
    loaded.passed(16)
    product.passed(nt)


def head_norm(k, name, src, n, width, gains, rope=None):
    nc = k.nc
    squared, mean, eps_added, root, normed = (k.sig(x) for x in ("hn_squared", "hn_mean", "hn_eps", "hn_root", "hn_normed"))
    rotated, turned = k.sig("hn_rotated"), k.sig("hn_turned", 2)
    roped = [i for i in range(n) if rope and rope[i]]
    with ExitStack() as c:
        sq = k.sb(c, name + "_sq", [P, n, width])
        t1 = k.sb(c, name + "_t1", [P, width])
        t2 = k.sb(c, name + "_t2", [P, width])
        ps = k.ps(c, name + "_ps", [P, 8, 512])
        block = c.enter_context(nc.Block())

        @block.scalar
        def _(act):
            act.activation(sq[:], src, ACT.Square).then_inc(squared.sem, 1)
            act.wait_ge(eps_added.sem, eps_added.done(0))
            act.activation(sq[:], sq[:], ACT.Sqrt).then_inc(root.sem, 1)

        @block.tensor
        def _(pe):
            pe.wait_ge(squared.sem, squared.done(0))
            for i in range(n):
                last = pe.matmul(ps[:, i, 0:width], k.col("headmean"), sq[:, i, :], start=True, stop=True)
            last.then_inc(mean.sem, 1)
            for m, i in enumerate(roped):
                pe.wait_ge(normed.sem, normed.done(i))
                pe.wait_ge(turned.sem, turned.free(m))
                pe.matmul(ps[:, m % 2, 0:width], k.col("rot"), src[:, i, :], start=True, stop=True).then_inc(rotated.sem, 1)

        @block.vector
        def _(dve):
            turned.give(dve)
            dve.wait_ge(mean.sem, mean.done(0))
            dve.tensor_scalar(sq[:], ps[:, 0:n, 0:width], EPS, None, ALU.add).then_inc(eps_added.sem, 1)
            dve.wait_ge(root.sem, root.done(0))
            dve.reciprocal(sq[:], sq[:])
            dve.drain()
            for i in range(n):
                dve.scalar_tensor_tensor(out=src[:, i, :], in0=src[:, i, :], scalar=gains[i], in1=sq[:, i, :],
                                         op0=ALU.mult, op1=ALU.mult).then_inc(normed.sem, 1)
            for m, i in enumerate(roped):
                cos, sin = rope[i]
                dve.wait_ge(rotated.sem, rotated.done(m))
                dve.tensor_tensor(t1[:], ps[:, m % 2, 0:width], sin, ALU.mult).then_inc(turned.sem, 1)
                dve.tensor_tensor(t2[:], src[:, i, :], cos, ALU.mult)
                dve.drain()
                dve.tensor_tensor(src[:, i, :], t1[:], t2[:], ALU.add)
                dve.drain()
    for s in (squared, mean, eps_added, root):
        s.passed(1)
    normed.passed(n)
    rotated.passed(len(roped))
    turned.passed(len(roped))


def rope_tables(k, cos, sin):
    nc = k.nc
    loaded, reduced = k.sig("rt_loaded"), k.sig("rt_reduced")
    two_pi = 2.0 * np.pi
    part1 = float(np.float32(6.28125))
    part2 = float(np.float32(np.float32((two_pi - part1) * 2 ** 20).astype(np.int32) >> 2 << 2) / np.float32(2 ** 20))
    part3 = float(np.float32(two_pi - part1 - part2))
    magic = 1.5 * 2.0 ** 23
    pi = float(np.nextafter(np.float32(np.pi), np.float32(0)))
    with ExitStack() as c:
        pos = k.sb(c, "rt_pos", [P, S], I32)
        ang = k.sb(c, "rt_ang", [P, S])
        turns = k.sb(c, "rt_turns", [P, S])
        block = c.enter_context(nc.Block())

        @block.sync
        def _(sp):
            sp.dma_start(pos[:], bc(k.dram["positions"].rearrange("(a n) -> a n", a=1), [P, S])).then_inc(loaded.sem, 16)

        @block.vector
        def _(dve):
            dve.wait_ge(loaded.sem, loaded.base + 16)
            dve.tensor_copy(ang[:], pos[:])
            dve.drain()
            dve.tensor_scalar(ang[:], ang[:], k.col("freq"), None, ALU.mult)
            dve.drain()
            for out, quarter in ((sin, 0.0), (cos, 0.25)):
                dve.tensor_scalar(turns[:], ang[:], 1.0 / two_pi, quarter, ALU.mult, ALU.add)
                dve.drain()
                dve.tensor_scalar(turns[:], turns[:], magic, None, ALU.add)
                dve.drain()
                dve.tensor_scalar(turns[:], turns[:], magic, None, ALU.subtract)
                dve.drain()
                dve.scalar_tensor_tensor(out=out[:], in0=turns[:], scalar=-part1, in1=ang[:], op0=ALU.mult, op1=ALU.add)
                dve.drain()
                dve.scalar_tensor_tensor(out=out[:], in0=turns[:], scalar=-part2, in1=out[:], op0=ALU.mult, op1=ALU.add)
                dve.drain()
                dve.scalar_tensor_tensor(out=out[:], in0=turns[:], scalar=-part3, in1=out[:], op0=ALU.mult, op1=ALU.add)
                dve.drain()
                if quarter:
                    dve.tensor_scalar(out[:], out[:], float(np.float32(np.pi / 2)), None, ALU.add)
                    dve.drain()
                dve.tensor_scalar(out[:], out[:], pi, -pi, ALU.min, ALU.max).then_inc(reduced.sem, 1)
                dve.drain()

        @block.scalar
        def _(act):
            for n, out in enumerate((sin, cos)):
                act.wait_ge(reduced.sem, reduced.done(n))
                act.activation(out[:], out[:], ACT.Sin)
    loaded.passed(16)
    reduced.passed(2)


def recurrent(k, proj, mixT):
    nc = k.nc
    gates_loaded, convolved, gated, opened = (k.sig(x) for x in ("rc_gates_loaded", "rc_conv", "rc_gated", "rc_opened"))
    decay_ready, exps, left_ready, rooted, gelu_ready = (k.sig(x) for x in ("rc_decay", "rc_exps", "rc_left", "rc_root", "rc_gelu"))
    freed = k.sig("rc_freed", 2)
    y_exp, y_ready = k.sig("rc_yexp"), k.sig("rc_y")
    n = LRU_CH
    with ExitStack() as c:
        gw = k.sb(c, "rc_gw", [P, n, 2, P])
        xc = k.sb(c, "rc_xc", [P, n, S])
        rec = k.sb(c, "rc_rec", [P, n, S])
        inp = k.sb(c, "rc_inp", [P, n, S])
        dec = k.sb(c, "rc_dec", [P, n, S])
        tnh = k.sb(c, "rc_tnh", [P, n, S])
        sp_ = k.sb(c, "rc_softplus", [P, 4, n])
        ps = k.ps(c, "rc_ps", [P, 2, 2, 512])
        block = c.enter_context(nc.Block())
        lam = k.col("lam")

        @block.sync
        def _(sp):
            sp.dma_start(gw[:], k.dram["gate_w"]).then_inc(gates_loaded.sem, 16)

        @block.tensor
        def _(pe):
            pe.wait_ge(gates_loaded.sem, gates_loaded.base + 16)
            for i in range(n):
                pe.wait_ge(convolved.sem, convolved.done(i))
                pe.wait_ge(freed.sem, freed.free(i))
                for g in range(2):
                    last = pe.matmul(ps[:, i % 2, g, :], gw[:, i, g, :], xc[:, i, :], start=True, stop=True)
                last.then_inc(gated.sem, 1)

        @block.scalar
        def _(act):
            freed.give(act)
            act.activation(sp_[:, 0, :], lam, ACT.Abs)
            act.drain()
            act.activation(sp_[:, 1, :], sp_[:, 0, :], ACT.Exp, scale=-1.0).then_inc(y_exp.sem, 1)
            for i in range(n):
                act.wait_ge(gated.sem, gated.done(i))
                act.activation(rec[:, i, :], ps[:, i % 2, 0, :], ACT.Sigmoid, bias=k.col("gate_b", i, 1)).then_inc(opened.sem, 1)
                act.activation(inp[:, i, :], ps[:, i % 2, 1, :], ACT.Sigmoid, bias=k.col("gate_b", n + i, 1)).then_inc(freed.sem, 1)
            act.wait_ge(decay_ready.sem, decay_ready.done(0))
            act.activation(dec[:], rec[:], ACT.Exp, scale=-1.0).then_inc(exps.sem, 1)
            act.activation(tnh[:], rec[:], ACT.Tanh).then_inc(exps.sem, 1)
            act.activation(proj[:, n:2 * n, :], proj[:, n:2 * n, :], ACT.Gelu_apprx_tanh).then_inc(gelu_ready.sem, 1)
            act.wait_ge(left_ready.sem, left_ready.done(0))
            act.activation(rec[:], rec[:], ACT.Sqrt).then_inc(rooted.sem, 1)

        @block.vector
        def _(dve):
            for i in range(n):
                dve.tensor_scalar(xc[:, i, :], proj[:, i, :], k.col("conv_w", 4 * i + 3, 1), k.col("conv_b", i, 1),
                                  ALU.mult, ALU.add)
                for s in (1, 2, 3):
                    dve.drain()
                    last = dve.scalar_tensor_tensor(out=xc[:, i, s:S], in0=proj[:, i, 0:S - s],
                                                    scalar=k.col("conv_w", 4 * i + 3 - s, 1), in1=xc[:, i, s:S],
                                                    op0=ALU.mult, op1=ALU.add)
                last.then_inc(convolved.sem, 1)
            y, s_, s2, acc = (sp_[:, j, :] for j in (1, 2, 0, 3))
            dve.wait_ge(y_exp.sem, y_exp.done(0))
            dve.tensor_scalar(s_, y, 2.0, None, ALU.add)
            dve.drain()
            dve.reciprocal(s_, s_)
            dve.drain()
            dve.tensor_tensor(s_, s_, y, ALU.mult)
            dve.drain()
            dve.tensor_tensor(s2, s_, s_, ALU.mult)
            dve.memset(acc, 1.0 / 19)
            dve.drain()
            for m in (17, 15, 13, 11, 9, 7, 5, 3, 1):
                dve.tensor_tensor(acc, acc, s2, ALU.mult)
                dve.drain()
                dve.tensor_scalar(acc, acc, 1.0 / m, None, ALU.add)
                dve.drain()
            dve.scalar_tensor_tensor(out=acc, in0=acc, scalar=2.0, in1=s_, op0=ALU.mult, op1=ALU.mult)
            dve.tensor_scalar(s2, lam, -1.0, 0.0, ALU.mult, ALU.max)
            dve.drain()
            dve.tensor_tensor(acc, acc, s2, ALU.add)
            dve.drain()
            dve.tensor_scalar(acc, acc, 8.0, None, ALU.mult)
            dve.drain()
            for i in range(n):
                dve.wait_ge(opened.sem, opened.done(i))
                last = dve.tensor_scalar(rec[:, i, :], rec[:, i, :], sp_[:, 3, i:i + 1], None, ALU.mult)
            last.then_inc(decay_ready.sem, 1)
            dve.wait_ge(freed.sem, freed.done(n - 1))
            dve.tensor_tensor(inp[:], inp[:], xc[:], ALU.mult)
            dve.wait_ge(exps.sem, exps.done(1))
            dve.drain()
            dve.tensor_tensor(xc[:], dec[:], dec[:], ALU.mult)
            dve.drain()
            dve.scalar_tensor_tensor(out=xc[:], in0=xc[:], scalar=1.0, in1=tnh[:], op0=ALU.add, op1=ALU.mult)
            dve.drain()
            dve.tensor_scalar(rec[:], xc[:], 1e-34, None, ALU.max).then_inc(left_ready.sem, 1)
            dve.wait_ge(rooted.sem, rooted.done(0))
            dve.tensor_tensor(inp[:], inp[:], rec[:], ALU.mult)
            dve.drain()
            for i in range(n):
                dve.tensor_tensor_scan(tnh[:, i, :], dec[:, i, :], inp[:, i, :], 0.0, ALU.mult, ALU.add)
            dve.wait_ge(gelu_ready.sem, gelu_ready.done(0))
            dve.drain()
            dve.tensor_tensor(mixT[:, 0:n, :], tnh[:], proj[:, n:2 * n, :], ALU.mult)
    gates_loaded.passed(16)
    for s in (convolved, gated, opened, freed):
        s.passed(n)
    for s in (decay_ready, left_ready, rooted, gelu_ready, y_exp):
        s.passed(1)
    exps.passed(2)


def attention(k, name, rounds, staged, units, o_out):
    nc = k.nc
    U = len(units)
    per_tile = U // TT
    R = 3
    copied, scored, maxed = k.sig("at_copied"), k.sig("at_scored"), k.sig("at_maxed")
    expd, scaled = k.sig("at_exp", R), k.sig("at_scaled")
    turned, stored = k.sig("at_turned", R), k.sig("at_stored", R)
    summed, out_done = k.sig("at_summed", R), k.sig("at_out", 2)
    copied_per = len(staged)
    with ExitStack() as c:
        prob = k.sb(c, name + "_p", [P, R, 512])
        probT = k.sb(c, name + "_pt", [P, R, 512])
        mx = k.sb(c, name + "_mx", [P, 4])
        nb = k.sb(c, name + "_nb", [P, 4])
        sm = k.sb(c, name + "_sm", [P, 4])
        rs = k.sb(c, name + "_rs", [P, 4])
        psS = k.ps(c, name + "_pss", [P, R, 512])
        psT = k.ps(c, name + "_pst", [P, R, 512])
        psO = k.ps(c, name + "_pso", [P, 2, 512])
        block = c.enter_context(nc.Block())

        @block.gpsimd
        def _(pool):
            with pool.Fori(0, rounds) as r:
                pool.wait_ge(out_done.sem, r * TT + out_done.base + 2)
                for dst, src in staged:
                    pool.tensor_copy(dst, src(r)).then_inc(copied.sem, 1)

        @block.tensor
        def _(pe):
            turned.give(pe)
            summed.give(pe)
            with pe.Fori(0, rounds) as r:
                pe.wait_ge(copied.sem, r * copied_per + copied.done(copied_per - 1))
                for step in range(U + 3):
                    if step < U:
                        half, t, keys, width, _, _, _ = units[step]
                        b = HD * half
                        pe.wait_ge(expd.sem, r * U + expd.free(step))
                        q = staged[0][0]
                        pe.matmul(psS[:, step % R, 0:width], q[b:b + HD, t * P:(t + 1) * P], keys[b:b + HD, 0:width],
                                  start=True, stop=True).then_inc(scored.sem, 1)
                    u = step - 2
                    if 0 <= u < U:
                        width = units[u][3]
                        pe.wait_ge(scaled.sem, r * U + scaled.done(u))
                        pe.wait_ge(stored.sem, r * U + stored.free(u))
                        for j in range(0, width, P):
                            w = min(P, width - j)
                            last = pe.transpose(psT[0:w, u % R, j:j + P], prob[:, u % R, j:j + w], k.col("ident"))
                        last.then_inc(turned.sem, 1)
                    u = step - 3
                    if 0 <= u < U:
                        half, t, _, width, _, _, values = units[u]
                        b = HD * half
                        of_head = [m for m in range(U) if units[m][0] == half and units[m][1] == t]
                        pe.wait_ge(stored.sem, r * U + stored.done(u))
                        if u % per_tile == 0:
                            pe.wait_ge(out_done.sem, r * TT + out_done.free(t))
                        blocks = range(0, width, P)
                        for j in blocks:
                            w = min(P, width - j)
                            last = pe.matmul(psO[b:b + HD, t % 2, 0:P], values(j // P), probT[0:w, u % R, j:j + P],
                                             start=(u == of_head[0] and j == 0),
                                             stop=(u == of_head[-1] and j == blocks[-1]))
                        last.then_inc(summed.sem, 1)

        @block.vector
        def _(dve):
            with dve.Fori(0, rounds) as r:
                for step in range(U + 1):
                    if step < U:
                        _, _, _, width, mask, _, _ = units[step]
                        dve.wait_ge(scored.sem, r * U + scored.done(step))
                        if mask is not None:
                            mw = mask.shape[1]
                            part = psS[:, step % R, width - mw:width]
                            dve.tensor_tensor(part, part, mask, ALU.add)
                            dve.drain()
                        dve.tensor_reduce(mx[:, step % 4:step % 4 + 1], psS[:, step % R, 0:width], AX.X, ALU.max)
                        dve.drain()
                        dve.tensor_scalar(nb[:, step % 4:step % 4 + 1], mx[:, step % 4:step % 4 + 1], -SCALE, None,
                                          ALU.mult).then_inc(maxed.sem, 1)
                    u = step - 1
                    if 0 <= u < U:
                        _, _, _, width, _, gate, _ = units[u]
                        dve.wait_ge(expd.sem, r * U + expd.done(u))
                        dve.reciprocal(rs[:, u % 4:u % 4 + 1], sm[:, u % 4:u % 4 + 1])
                        dve.drain()
                        if gate is not None and u == 0:
                            dve.wait_ge(copied.sem, r * copied_per + copied.done(copied_per - 1))
                        if gate is None:
                            dve.tensor_scalar(prob[:, u % R, 0:width], prob[:, u % R, 0:width], rs[:, u % 4:u % 4 + 1],
                                              None, ALU.mult).then_inc(scaled.sem, 1)
                        else:
                            dve.tensor_scalar(prob[:, u % R, 0:width], prob[:, u % R, 0:width], rs[:, u % 4:u % 4 + 1],
                                              gate, ALU.mult, ALU.mult).then_inc(scaled.sem, 1)

        @block.scalar
        def _(act):
            expd.give(act)
            stored.give(act)
            out_done.give(act)
            with act.Fori(0, rounds) as r:
                for step in range(U + 4):
                    if step < U:
                        width = units[step][3]
                        act.wait_ge(maxed.sem, r * U + maxed.done(step))
                        act.wait_ge(turned.sem, r * U + turned.free(step))
                        act.activation(prob[:, step % R, 0:width], psS[:, step % R, 0:width], ACT.Exp,
                                       bias=nb[:, step % 4:step % 4 + 1], scale=SCALE,
                                       accum_out=sm[:, step % 4:step % 4 + 1]).then_inc(expd.sem, 1)
                    u = step - 2
                    if 0 <= u < U:
                        width = units[u][3]
                        w = min(width, P)
                        act.wait_ge(turned.sem, r * U + turned.done(u))
                        act.wait_ge(summed.sem, r * U + summed.free(u))
                        act.activation(probT[0:w, u % R, 0:max(width, P)], psT[0:w, u % R, 0:max(width, P)],
                                       ACT.Copy).then_inc(stored.sem, 1)
                    u = step - 4
                    if 0 <= u < U and u % per_tile == per_tile - 1:
                        t = units[u][1]
                        act.wait_ge(summed.sem, r * U + summed.done(u))
                        act.activation(o_out(r, t), psO[:, t % 2, 0:P], ACT.Copy).then_inc(out_done.sem, 1)
    copied.passed(copied_per * rounds)
    for s in (scored, maxed, expd, scaled, turned, stored, summed):
        s.passed(U * rounds)
    out_done.passed(TT * rounds)


def memory_attention(k, l, qm, mixT):
    with ExitStack() as c:
        kT = k.sb(c, f"ma_kT{l}", [P, MEM_CH, MEMLEN])
        v = k.sb(c, f"ma_v{l}", [P, MT, 2 * P])
        with ExitStack() as c2:
            mem = k.sb(c2, f"ma_mem{l}", [P, MT, D])
            memT = k.sb(c2, f"ma_memT{l}", [P, DC, MEMLEN])
            load(k, "mem", [(mem[:], k.dram["mem"].rearrange("(t p) d -> p t d", p=P))])
            norm_transpose(k, f"ma_n{l}", mem, MT, k.col(f"norm_mem{l}"), memT)
            project(k, f"ma_k{l}", k.dram[f"w_mem_k{l}"], MEM_CH, memT[:], MEMLEN, kT)
            natural(k, f"ma_vp{l}", k.dram[f"w_mem_v{l}"], 2 * P, memT, MT, v)
        head_norm(k, f"ma_kn{l}", kT[:], MEM_CH, MEMLEN, [k.col(f"mk_gain{l}")] * MEM_CH)
        head_norm(k, f"ma_qn{l}", qm, MEM_CH, S, [k.col(f"mq_gain{l}")] * MEM_CH)
        q_now = k.sb(c, f"ma_qs{l}", [P, S])
        k_now = k.sb(c, f"ma_ks{l}", [P, MEMLEN])
        v_now = k.sb(c, f"ma_vs{l}", [P, MT, P])
        units = [(half, t, k_now, MEMLEN, None, None, (lambda j, half=half: v_now[:, j, half * HD:(half + 1) * HD]))
                 for t in range(TT) for half in range(2)]
        staged = [
            (q_now[:], lambda r: qm[:, bass.ds(r, 1), :].rearrange("p a n -> p (a n)")),
            (k_now[:], lambda r: kT[:, bass.ds(r, 1), :].rearrange("p a n -> p (a n)")),
            (v_now[:], lambda r: v[:, :, bass.ds(r * P, P)]),
        ]
        attention(k, f"ma_at{l}", MEM_CH, staged, units,
                  lambda r, t: mixT[:, bass.ds(r + LRU_CH, 1), t * P:(t + 1) * P].rearrange("p a n -> p (a n)"))


def out_project(k, l, mixT, x):
    nc = k.nc
    loaded, product, added = k.sig("op_loaded"), k.sig("op_product"), k.sig("op_added", 4)
    with ExitStack() as c:
        w = k.sb(c, f"op_w{l}", [P, DC, D])
        ps = k.ps(c, f"op_ps{l}", [P, 4, 512])
        block = c.enter_context(nc.Block())

        @block.sync
        def _(sp):
            sp.dma_start(w[:], k.dram[f"w_out{l}"].rearrange("(c p) d -> p c d", p=P)).then_inc(loaded.sem, 16)

        @block.tensor
        def _(pe):
            pe.wait_ge(loaded.sem, loaded.base + 16)
            for n in range(2 * TT):
                t, h = n // 2, n % 2
                pe.wait_ge(added.sem, added.free(n))
                for dc in range(DC):
                    last = pe.matmul(ps[:, n % 4, :], mixT[:, dc, t * P:(t + 1) * P], w[:, dc, h * 512:(h + 1) * 512],
                                     start=(dc == 0), stop=(dc == DC - 1))
                last.then_inc(product.sem, 1)

        @block.vector
        def _(dve):
            added.give(dve)
            for n in range(2 * TT):
                t, h = n // 2, n % 2
                dve.wait_ge(product.sem, product.done(n))
                part = x[:, t, h * 512:(h + 1) * 512]
                dve.tensor_tensor(part, part, ps[:, n % 4, :], ALU.add).then_inc(added.sem, 1)
    loaded.passed(16)
    product.passed(2 * TT)
    added.passed(2 * TT)


def compress(k, tok, cos, sin, kc, vc):
    nc = k.nc
    loaded, blocked, hidden, acted, outd = (k.sig(x) for x in ("cp_loaded", "cp_blocked", "cp_hidden", "cp_acted", "cp_out"))
    LP = CMP_LEN // 2
    with ExitStack() as c:
        w1 = k.sb(c, "cp_w1", [P, 2, LP, HID])
        w2 = k.sb(c, "cp_w2", [P, 2, 2, HD])
        blk = k.sb(c, "cp_blk", [P, 2, LP, 2, CMPW])
        hid = k.sb(c, "cp_hid", [P, 2, 2, 2 * CMPW])
        ps = k.ps(c, "cp_ps", [P, 4, 512])
        psk = k.ps(c, "cp_psk", [P, 512])
        psv = k.ps(c, "cp_psv", [P, 512])
        with nc.Block() as block:
            @block.sync
            def _(sp):
                for j in range(2):
                    sp.dma_start(w1[:, j, :, :], k.dram["cmp_w1"][j].rearrange("(c p) h -> p c h", p=P)).then_inc(loaded.sem, 16)
                    sp.dma_start(w2[:, j, :, :], k.dram["cmp_w2"][j].rearrange("(c p) h -> p c h", p=P)).then_inc(loaded.sem, 16)

            @block.vector
            def _(dve):
                dve.memset(blk[:], 0.0)
                dve.drain()
                for j in range(2):
                    for g in range(2):
                        for l2 in range(2):
                            rows = slice(l2 * HD, (l2 + 1) * HD)
                            by_step = tok[rows, 2 * j + g, :].rearrange("p (n s) -> p s n", s=CMP_STRIDE)
                            for hi in range(2):
                                pos = k.col("cmp_pos", LP * j + 8 * hi, 8)[rows, :]
                                last = dve.tensor_tensor(blk[rows, j, 8 * hi:8 * hi + 8, g, 0:N_CMP],
                                                         by_step[:, l2::2, hi:hi + N_CMP],
                                                         bc(pos.unsqueeze(2), [HD, 8, N_CMP]), ALU.add)
                dve.drain()
                dve.memset(kc[:], 0.0).then_inc(blocked.sem, 1)

            @block.tensor
            def _(pe):
                pe.wait_ge(loaded.sem, loaded.base + 64)
                pe.wait_ge(blocked.sem, blocked.done(0))
                for j in range(2):
                    for h in range(2):
                        for lp in range(LP):
                            last = pe.matmul(ps[:, 2 * j + h, 0:2 * CMPW], w1[:, j, lp, h * P:(h + 1) * P],
                                             blk[:, j, lp, :, :], start=(lp == 0), stop=(lp == LP - 1))
                        last.then_inc(hidden.sem, 1)
                pe.wait_ge(acted.sem, acted.done(3))
                for g in range(2):
                    for h in range(2):
                        last = pe.matmul(psk[g * HD:(g + 1) * HD, 0:CMPW], w2[:, 0, h, :],
                                         hid[:, 0, h, g * CMPW:(g + 1) * CMPW], start=(h == 0), stop=(h == 1))
                last.then_inc(outd.sem, 1)
                for g in range(2):
                    for h in range(2):
                        last = pe.matmul(psv[0:CMPW, g * HD:(g + 1) * HD], hid[:, 1, h, g * CMPW:(g + 1) * CMPW],
                                         w2[:, 1, h, :], start=(h == 0), stop=(h == 1))
                last.then_inc(outd.sem, 1)

            @block.scalar
            def _(act):
                for n in range(4):
                    act.wait_ge(hidden.sem, hidden.done(n))
                    act.activation(hid[:, n // 2, n % 2, :], ps[:, n, 0:2 * CMPW], ACT.Gelu_apprx_tanh,
                                   bias=k.col("cmp_b1", n, 1)).then_inc(acted.sem, 1)
                act.wait_ge(outd.sem, outd.done(1))
                act.activation(kc[:, 0, 0:N_CMP], psk[:, 0:N_CMP], ACT.Copy)
                act.activation(vc[0:CMPW, :], psv[0:CMPW, 0:2 * HD], ACT.Copy)
    loaded.passed(64)
    blocked.passed(1)
    hidden.passed(4)
    acted.passed(4)
    outd.passed(2)
    at_block_end = lambda table: table[:].rearrange("p (n s) -> p n s", s=CMP_STRIDE)[:, 1:N_CMP + 1, CMP_STRIDE - 1]
    head_norm(k, "cp_hn", kc[:, :, 0:N_CMP], 1, N_CMP, [k.col("k_gain", 0, 1)], [(at_block_end(cos), at_block_end(sin))])


def nsa_gates(k, gates):
    nc = k.nc
    biased, opened = k.sig("ng_biased"), k.sig("ng_opened")
    with nc.Block() as block:
        @block.vector
        def _(dve):
            dve.tensor_tensor(gates[:], gates[:], bc(k.col("nsa_gate_b").unsqueeze(1), [P, TT, 36]), ALU.add).then_inc(biased.sem, 1)
            dve.wait_ge(opened.sem, opened.done(0))
            cmp0 = gates[:, 0, :].rearrange("p (h b) -> p h b", b=3)[:, :, 0]
            dve.tensor_scalar(cmp0, cmp0, k.col("rowvalid"), None, ALU.mult)

        @block.scalar
        def _(act):
            act.wait_ge(biased.sem, biased.done(0))
            act.activation(gates[:], gates[:], ACT.Sigmoid).then_inc(opened.sem, 1)
    biased.passed(1)
    opened.passed(1)


def route(k, l, hT, valsb, key1, key2):
    nc = k.nc
    wq_loaded = [k.sig("ro_wq0"), k.sig("ro_wq1")]
    sk_loaded = [k.sig("ro_sk0"), k.sig("ro_sk1")]
    queried, q_stored, scored, s_stored = k.sig("ro_queried", 2), k.sig("ro_qstored", 2), k.sig("ro_scored", 2), k.sig("ro_sstored", 2)
    selected = k.sig("ro_selected", 1)
    with ExitStack() as c:
        wq = k.sb(c, f"ro_wq{l}", [P, 2, DC, P])
        sk = k.sb(c, f"ro_sk{l}", [P, 2, NK])
        q = k.sb(c, f"ro_q{l}", [P, 2, S])
        sc = k.sb(c, f"ro_s{l}", [P, 2, TT, NK])
        sc2 = k.sb(c, f"ro_s2{l}", [P, 2, TT, NK])
        top = k.sb(c, f"ro_top{l}", [P, 2, TT, TOPK])
        idx = k.sb(c, f"ro_idx{l}", [P, 2, TT, TOPK], U32)
        idxf = k.sb(c, f"ro_idxf{l}", [P, 2, TT, TOPK])
        cand = k.sb(c, f"ro_cand{l}", [P, TT, TOPK, TOPK])
        cand2 = k.sb(c, f"ro_cand2{l}", [P, TT, TOPK * TOPK])
        best = k.sb(c, f"ro_best{l}", [P, TT, TOPK])
        ci = k.sb(c, f"ro_ci{l}", [P, TT, TOPK], U32)
        pick = k.sb(c, f"ro_pick{l}", [P, 2, TT, TOPK], U32)
        pickf = k.sb(c, f"ro_pickf{l}", [P, 2, TT, TOPK])
        hot = k.sb(c, f"ro_hot{l}", [P, TT * TOPK, TOPK])
        keys = k.sb(c, f"ro_keys{l}", [P, 2, TT, TOPK])
        psq = k.ps(c, f"ro_psq{l}", [P, 2, 512])
        pss = k.ps(c, f"ro_pss{l}", [P, 2, TT, P])
        block = c.enter_context(nc.Block())
        w, subkeys = k.dram[f"peer_wq{l}"], k.dram[f"subkeys{l}"]

        @block.sync
        def _(sp):
            with sp.Fori(0, PH) as h:
                for b in range(2):
                    sp.wait_ge(queried.sem, h * 2 + queried.free(b))
                    sp.dma_start(wq[:, b, :, :], w[bass.ds(h * 2 + b, 1), :, :, :].rearrange("a p c m -> p (a c) m")
                                 ).then_inc(wq_loaded[b].sem, 16)
                    sp.wait_ge(scored.sem, h * 2 + scored.free(b))
                    sp.dma_start(sk[:, b, :], subkeys[bass.ds(h * 2 + b, 1), :, :].rearrange("a p n -> p (a n)")
                                 ).then_inc(sk_loaded[b].sem, 16)

        @block.tensor
        def _(pe):
            queried.give(pe)
            scored.give(pe)
            with pe.Fori(0, PH) as h:
                for b in range(2):
                    pe.wait_ge(wq_loaded[b].sem, h * 16 + wq_loaded[b].base + 16)
                    pe.wait_ge(q_stored.sem, h * 2 + q_stored.free(b))
                    for dc in range(DC):
                        last = pe.matmul(psq[:, b, :], wq[:, b, dc, :], hT[:, dc, :], start=(dc == 0), stop=(dc == DC - 1))
                    last.then_inc(queried.sem, 1)
                for b in range(2):
                    pe.wait_ge(sk_loaded[b].sem, h * 16 + sk_loaded[b].base + 16)
                    pe.wait_ge(q_stored.sem, h * 2 + q_stored.done(b))
                    pe.wait_ge(s_stored.sem, h * 2 + s_stored.free(b))
                    for t in range(TT):
                        last = pe.matmul(pss[:, b, t, :], q[:, b, t * P:(t + 1) * P], sk[:, b, :], start=True, stop=True)
                    last.then_inc(scored.sem, 1)

        @block.scalar
        def _(act):
            q_stored.give(act)
            s_stored.give(act)
            with act.Fori(0, PH) as h:
                for b in range(2):
                    act.wait_ge(queried.sem, h * 2 + queried.done(b))
                    act.wait_ge(scored.sem, h * 2 + scored.free(b))
                    act.activation(q[:, b, :], psq[:, b, :], ACT.Copy).then_inc(q_stored.sem, 1)
                act.wait_ge(selected.sem, h + selected.free(0))
                for b in range(2):
                    act.wait_ge(scored.sem, h * 2 + scored.done(b))
                    act.activation(sc[:, b, :, :], pss[:, b, :, :], ACT.Copy).then_inc(s_stored.sem, 1)

        @block.vector
        def _(dve):
            selected.give(dve)
            with dve.Fori(0, PH) as h:
                dve.wait_ge(s_stored.sem, h * 2 + s_stored.done(1))
                dve.memset(hot[:, 0, 0:1], 0.0)
                pairs = [(b, t) for b in range(2) for t in range(TT)]
                for b, t in pairs:
                    dve.max(top[:, b, t, 0:8], sc[:, b, t, :])
                dve.drain()
                for b, t in pairs:
                    dve.max_index(idx[:, b, t, 0:8], top[:, b, t, 0:8], sc[:, b, t, :])
                    dve.match_replace(sc2[:, b, t, :], top[:, b, t, 0:8], sc[:, b, t, :], -3.0e38)
                dve.drain()
                for b, t in pairs:
                    dve.max(top[:, b, t, 8:16], sc2[:, b, t, :])
                dve.drain()
                for b, t in pairs:
                    dve.max_index(idx[:, b, t, 8:16], top[:, b, t, 8:16], sc2[:, b, t, :])
                dve.drain()
                dve.tensor_copy(idxf[:], idx[:])
                for t in range(TT):
                    dve.tensor_tensor(cand[:, t, :, :], bc(top[:, 0, t, :].unsqueeze(2), [P, TOPK, TOPK]),
                                      bc(top[:, 1, t, :].unsqueeze(1), [P, TOPK, TOPK]), ALU.add)
                dve.drain()
                flat = cand[:].rearrange("p t a b -> p t (a b)")
                for t in range(TT):
                    dve.max(best[:, t, 0:8], flat[:, t, :])
                dve.drain()
                for t in range(TT):
                    dve.max_index(ci[:, t, 0:8], best[:, t, 0:8], flat[:, t, :])
                    dve.match_replace(cand2[:, t, :], best[:, t, 0:8], flat[:, t, :], -3.0e38)
                dve.drain()
                for t in range(TT):
                    dve.max(best[:, t, 8:16], cand2[:, t, :])
                dve.drain()
                for t in range(TT):
                    dve.max_index(ci[:, t, 8:16], best[:, t, 8:16], cand2[:, t, :])
                dve.drain()
                dve.tensor_scalar(pick[:, 0, :, :], ci[:], 4, None, ALU.logical_shift_right)
                dve.tensor_scalar(pick[:, 1, :, :], ci[:], 15, None, ALU.bitwise_and)
                dve.drain()
                dve.tensor_copy(pickf[:], pick[:])
                dve.drain()
                iota = bc(k.col("iota", 0, TOPK).unsqueeze(1), [P, TT * TOPK, TOPK])
                for b in range(2):
                    dve.tensor_tensor(hot[:], bc(pickf[:, b, :, :].rearrange("p t k -> p (t k)").unsqueeze(2),
                                                 [P, TT * TOPK, TOPK]), iota, ALU.is_equal)
                    dve.drain()
                    hot4 = hot[:].rearrange("p (t k) a -> p t k a", t=TT)
                    dve.tensor_tensor(hot4, hot4, bc(idxf[:, b, :, :].unsqueeze(2), [P, TT, TOPK, TOPK]), ALU.mult)
                    dve.drain()
                    dve.tensor_reduce(keys[:, b, :, :].rearrange("p t k -> p (t k)"), hot[:], AX.X, ALU.add)
                    dve.drain()
                at = bass.ds(h * TOPK, TOPK)
                dve.tensor_copy(key1[:, :, at], keys[:, 0, :, :])
                dve.tensor_copy(key2[:, :, at], keys[:, 1, :, :])
                dve.tensor_copy(valsb[:, :, at], best[:]).then_inc(selected.sem, 1)
                dve.drain()
    for s in (*wq_loaded, *sk_loaded):
        s.passed(16 * PH)
    for s in (queried, q_stored, scored, s_stored):
        s.passed(2 * PH)
    selected.passed(PH)


def gate_softmax(k, l, vals, key1, key2, rows):
    nc = k.nc
    shifted, expd, ready, turned = (k.sig(x) for x in ("gs_shifted", "gs_exp", "gs_ready", "gs_turned"))
    with ExitStack() as c:
        total = k.sb(c, f"gs_total{l}", [P, TT * PH])
        ps = k.ps(c, f"gs_ps{l}", [P, 3, TT, P])
        block = c.enter_context(nc.Block())
        by_head = vals[:].rearrange("p t (h k) -> p (t h) k", k=TOPK)
        n = TT * PH

        @block.vector
        def _(dve):
            dve.tensor_copy(total[:].unsqueeze(2), by_head[:, :, 0:1])
            dve.drain()
            dve.tensor_tensor(by_head, by_head, bc(total[:].unsqueeze(2), [P, n, TOPK]), ALU.subtract).then_inc(shifted.sem, 1)
            dve.wait_ge(expd.sem, expd.done(0))
            dve.tensor_reduce(total[:], by_head, AX.X, ALU.add)
            dve.drain()
            dve.reciprocal(total[:], total[:])
            dve.drain()
            dve.tensor_tensor(by_head, by_head, bc(total[:].unsqueeze(2), [P, n, TOPK]), ALU.mult).then_inc(ready.sem, 1)
            for j in range(3):
                dve.wait_ge(turned.sem, turned.done(j))
                dve.tensor_copy(rows[:, j, :], ps[:, j, :, :].rearrange("p t n -> p (t n)"))

        @block.scalar
        def _(act):
            act.wait_ge(shifted.sem, shifted.done(0))
            act.activation(vals[:], vals[:], ACT.Exp).then_inc(expd.sem, 1)

        @block.tensor
        def _(pe):
            pe.wait_ge(ready.sem, ready.done(0))
            for j, src in enumerate((key1, key2, vals)):
                for t in range(TT):
                    last = pe.transpose(ps[:, j, t, :], src[:, t, :], k.col("ident"))
                last.then_inc(turned.sem, 1)
    for s in (shifted, expd, ready):
        s.passed(1)
    turned.passed(3)


def spread_gates(k, l, rows, gmat):
    nc = k.nc
    staged, spread, stored, written = k.sig("sg_staged"), k.sig("sg_spread", 4), k.sig("sg_stored", 4), k.sig("sg_written", 16)
    Q = 4
    NQ = TB // Q
    R = 4
    with ExitStack() as c:
        now = k.sb(c, f"sg_now{l}", [P, 3, TB])
        left = k.sb(c, f"sg_left{l}", [P, R, Q, NK])
        right = k.sb(c, f"sg_right{l}", [P, R, Q, NK])
        gbuf = k.sb(c, f"sg_gbuf{l}", [P, NK, TB])
        ps = k.ps(c, f"sg_ps{l}", [P, R, Q, NK])
        block = c.enter_context(nc.Block())
        iota = k.col("iota")

        @block.vector
        def _(dve):
            with dve.Fori(0, NTB) as blk:
                dve.drain()
                dve.tensor_copy(now[:], rows[:, :, bass.ds(blk * TB, TB)])
                dve.drain()
                for n in range(NQ):
                    dve.wait_ge(spread.sem, blk * NQ + spread.free(n))
                    for j in range(Q):
                        t = n * Q + j
                        dve.tensor_scalar(left[:, n % R, j, :], iota, now[:, 1, t:t + 1], None, ALU.is_equal)
                        last = dve.tensor_scalar(right[:, n % R, j, :], iota, now[:, 0, t:t + 1], now[:, 2, t:t + 1],
                                                 ALU.is_equal, ALU.mult)
                    last.then_inc(staged.sem, 1)

        @block.tensor
        def _(pe):
            spread.give(pe)
            with pe.Fori(0, NTB) as blk:
                for n in range(NQ):
                    pe.wait_ge(staged.sem, blk * NQ + staged.done(n))
                    pe.wait_ge(stored.sem, blk * NQ + stored.free(n))
                    for j in range(Q):
                        last = pe.matmul(ps[:, n % R, j, :], left[:, n % R, j, :], right[:, n % R, j, :], start=True, stop=True)
                    last.then_inc(spread.sem, 1)

        @block.scalar
        def _(act):
            stored.give(act)
            with act.Fori(0, NTB) as blk:
                act.wait_ge(written.sem, blk * 16 + written.free(15))
                for n in range(NQ):
                    act.wait_ge(spread.sem, blk * NQ + spread.done(n))
                    act.activation(gbuf[:, :, n * Q:(n + 1) * Q].rearrange("p i t -> p t i"), ps[:, n % R, :, :],
                                   ACT.Copy).then_inc(stored.sem, 1)

        @block.sync
        def _(sp):
            written.give(sp)
            with sp.Fori(0, NTB) as blk:
                sp.wait_ge(stored.sem, blk * NQ + stored.done(NQ - 1))
                sp.dma_start(gmat[:, bass.ds(blk, 1), :, :].rearrange("p a i t -> p (a i t)"),
                             gbuf[:].rearrange("p i t -> p (i t)")).then_inc(written.sem, 16)
            sp.wait_ge(written.sem, written.done(16 * NTB - 1))
    for s in (staged, spread, stored):
        s.passed(NTB * NQ)
    written.passed(16 * NTB)


def experts(k, l, hT, x, gmat):
    nc = k.nc
    u_loaded = [k.sig("ex_uload0"), k.sig("ex_uload1")]
    v_loaded = [k.sig("ex_vload0"), k.sig("ex_vload1")]
    g_loaded = [k.sig("ex_gload0"), k.sig("ex_gload1")]
    u_hi, u_lo = k.sig("ex_uhi"), k.sig("ex_ulo", 2)
    v_hi, v_lo = k.sig("ex_vhi"), k.sig("ex_vlo", 2)
    dots, gelued = k.sig("ex_dots", 2), k.sig("ex_gelu", 2)
    weighted, ready = k.sig("ex_weighted", 2), k.sig("ex_ready", 2)
    summed, added = k.sig("ex_summed"), k.sig("ex_added", 4)
    NO = 2 * TT
    with ExitStack() as c:
        hhi = k.sb(c, f"ex_hhi{l}", [P, DC, S], F32R)
        hlo = k.sb(c, f"ex_hlo{l}", [P, DC, S], F32R)
        ur = k.sb(c, f"ex_ur{l}", [P, 2, DC, P])
        uh = k.sb(c, f"ex_uh{l}", [P, 2, DC, P], F32R)
        ul = k.sb(c, f"ex_ul{l}", [P, 2, DC, P], F32R)
        vr = k.sb(c, f"ex_vr{l}", [P, 2, D])
        vh = k.sb(c, f"ex_vh{l}", [P, 2, GT, D], F32R)
        vl = k.sb(c, f"ex_vl{l}", [P, 2, GT, D], F32R)
        gm = k.sb(c, f"ex_gm{l}", [P, 2, NTB, GT, TB])
        act_ = k.sb(c, f"ex_act{l}", [P, 2, S])
        ah = k.sb(c, f"ex_ah{l}", [P, 2, GT, S], F32R)
        al = k.sb(c, f"ex_al{l}", [P, 2, GT, S], F32R)
        psz = k.ps(c, f"ex_psz{l}", [P, 2, 512])
        psy = k.ps(c, f"ex_psy{l}", [P, 4, 512])
        hi_ready = k.sig("ex_hhi")
        with nc.Block() as block:
            @block.scalar
            def _(act):
                act.activation(hhi[:], hT[:], ACT.Copy).then_inc(hi_ready.sem, 1)

            @block.vector
            def _(dve):
                dve.wait_ge(hi_ready.sem, hi_ready.done(0))
                dve.tensor_tensor(hlo[:], hT[:], hhi[:].bitcast(F32), ALU.subtract)
        hi_ready.passed(1)
        block = c.enter_context(nc.Block())
        u_d, v_d = k.dram[f"uT{l}"], k.dram[f"v{l}"]

        @block.sync
        def _(sp):
            def load_u(tile, a):
                sp.wait_ge(u_lo.sem, tile + u_lo.free(0))
                sp.dma_start(ur[:, a, :, :].unsqueeze(1), u_d[bass.ds(tile, 1), :, :, :].rearrange("a p c e -> p a c e")
                             ).then_inc(u_loaded[a].sem, 16)

            def load_v(tile, a):
                sp.wait_ge(v_lo.sem, tile + v_lo.free(0))
                sp.dma_start(vr[:, a, :], v_d[bass.ds(tile * P, P), :]).then_inc(v_loaded[a].sem, 16)

            def load_g(g, par):
                sp.wait_ge(ready.sem, g + ready.free(0))
                sp.dma_start(gm[:, par, :, :, :].rearrange("p b i t -> p b (i t)"),
                             gmat[:, :, bass.ds(g * GT, GT), :].rearrange("p b i t -> p b (i t)")
                             ).then_inc(g_loaded[par].sem, 16)

            with sp.Fori(0, NG // 2) as i:
                for par in range(2):
                    load_g(i * 2 + par, par)
                    for a in range(GT):
                        load_u(i * (2 * GT) + (par * GT + a), a)
                        load_v(i * (2 * GT) + (par * GT + a), a)

        @block.tensor
        def _(pe):
            dots.give(pe)

            def u_products(g):
                for a in range(GT):
                    pe.wait_ge(u_lo.sem, g * GT + u_lo.done(a))
                    pe.wait_ge(gelued.sem, g * GT + gelued.free(a))
                    for dc in range(DC):
                        for m, (w, h) in enumerate(((uh, hhi), (uh, hlo), (ul, hhi))):
                            last = pe.matmul(psz[:, a, :], w[:, a, dc, :], h[:, dc, :], start=(dc == 0 and m == 0),
                                             stop=(dc == DC - 1 and m == 2))
                    last.then_inc(dots.sem, 1)

            def v_products(g, par):
                pe.wait_ge(ready.sem, g + ready.done(0))
                for o in range(NO):
                    t, h = o // 2, o % 2
                    cols, toks = slice(h * 512, (h + 1) * 512), slice(t * P, (t + 1) * P)
                    pe.wait_ge(added.sem, g * NO + added.free(o))
                    for a in range(GT):
                        for m, (w, v) in enumerate(((ah, vh), (ah, vl), (al, vh))):
                            last = pe.matmul(psy[:, o % 4, :], w[:, par, a, toks], v[:, par, a, cols],
                                             start=(a == 0 and m == 0), stop=(a == GT - 1 and m == 2))
                    last.then_inc(summed.sem, 1)

            u_products(0)
            with pe.Fori(0, NG // 2 - 1) as i:
                u_products(i * 2 + 1)
                v_products(i * 2, 0)
                u_products(i * 2 + 2)
                v_products(i * 2 + 1, 1)
            u_products(NG - 1)
            v_products(NG - 2, 0)
            v_products(NG - 1, 1)

        @block.scalar
        def _(act):
            gelued.give(act)

            def u_high(tile, a, n16):
                act.wait_ge(u_loaded[a].sem, n16)
                act.wait_ge(dots.sem, tile + dots.free(0))
                act.activation(uh[:, a, :, :], ur[:, a, :, :], ACT.Copy).then_inc(u_hi.sem, 1)

            def v_high(a, par, n16):
                act.wait_ge(v_loaded[a].sem, n16)
                act.activation(vh[:, par, a, :], vr[:, a, :], ACT.Copy).then_inc(v_hi.sem, 1)

            def step(g, par, more=True):
                for a in range(GT):
                    v_high(a, par, g * 16 + v_loaded[a].base + 16)
                for a in range(GT):
                    act.wait_ge(dots.sem, g * GT + dots.done(a))
                    act.wait_ge(weighted.sem, g * GT + weighted.free(a))
                    act.activation(act_[:, a, :], psz[:, a, :], ACT.Gelu_apprx_tanh).then_inc(gelued.sem, 1)
                    if more:
                        u_high(g * GT + (GT + a), a, g * 16 + u_loaded[a].base + 32)

            def wait_half(g):
                act.wait_ge(summed.sem, g * NO + summed.base)

            for a in range(GT):
                u_high(a, a, u_loaded[a].base + 16)
            step(0, 0)
            step(1, 1)
            with act.Fori(1, NG // 2 - 1) as i:
                wait_half(i * 2 - 1)
                step(i * 2, 0)
                wait_half(i * 2)
                step(i * 2 + 1, 1)
            wait_half(NG - 3)
            step(NG - 2, 0)
            wait_half(NG - 2)
            step(NG - 1, 1, more=False)

        @block.vector
        def _(dve):
            u_lo.give(dve)
            v_lo.give(dve)
            weighted.give(dve)
            ready.give(dve)
            added.give(dve)

            def u_low(tile, a):
                dve.wait_ge(u_hi.sem, tile + u_hi.done(0))
                dve.tensor_tensor(ul[:, a, :, :], ur[:, a, :, :], uh[:, a, :, :].bitcast(F32), ALU.subtract).then_inc(u_lo.sem, 1)

            def v_low(tile, a, par):
                dve.wait_ge(v_hi.sem, tile + v_hi.done(0))
                dve.tensor_tensor(vl[:, par, a, :], vr[:, a, :], vh[:, par, a, :].bitcast(F32), ALU.subtract).then_inc(v_lo.sem, 1)

            def weigh(g, a, par):
                if a == 0:
                    dve.wait_ge(g_loaded[par].sem, g_need(g, par))
                dve.wait_ge(gelued.sem, g * GT + gelued.done(a))
                blocks = act_[:, a, :].rearrange("p (b t) -> p b t", t=TB)
                dve.tensor_tensor(blocks, blocks, gm[:, par, :, a, :], ALU.mult)
                dve.drain()
                dve.tensor_copy(ah[:, par, a, :], act_[:, a, :])
                dve.drain()
                last = dve.tensor_tensor(al[:, par, a, :], act_[:, a, :], ah[:, par, a, :].bitcast(F32), ALU.subtract)
                last.then_inc(weighted.sem, 1)
                if a == GT - 1:
                    dve.wait_ge(weighted.sem, g * GT + weighted.done(a))
                    dve.sem_inc(ready.sem, 1)

            def g_need(g, par):
                return g * 8 + (g_loaded[par].base + 16 - 8 * par)

            def add(g, n):
                dve.drain()
                for o in n:
                    t, h = o // 2, o % 2
                    dve.wait_ge(summed.sem, g * NO + summed.done(o))
                    part = x[:, t, h * 512:(h + 1) * 512]
                    dve.tensor_tensor(part, part, psy[:, o % 4, :], ALU.add).then_inc(added.sem, 1)

            def step(g, par, adds=True, more=True):
                for a in range(GT):
                    v_low(g * GT + a, a, par)
                weigh(g, 0, par)
                if more:
                    u_low(g * GT + GT, 0)
                weigh(g, 1, par)
                if adds:
                    add(g - 1, range(0, NO // 2))
                if more:
                    u_low(g * GT + (GT + 1), 1)
                if adds:
                    add(g - 1, range(NO // 2, NO))

            for a in range(GT):
                u_low(a, a)
            step(0, 0, adds=False)
            step(1, 1)
            with dve.Fori(1, NG // 2 - 1) as i:
                step(i * 2, 0)
                step(i * 2 + 1, 1)
            step(NG - 2, 0)
            step(NG - 1, 1, more=False)
            add(NG - 1, range(NO))
    for s in (*u_loaded, *v_loaded):
        s.passed(16 * NG)
    for s in g_loaded:
        s.passed(8 * NG)
    for s in (u_hi, u_lo, v_hi, v_lo, dots, gelued, weighted):
        s.passed(NK)
    ready.passed(NG)
    summed.passed(NG * NO)
    added.passed(NG * NO)


def peer(k, l, x, gmat):
    with ExitStack() as c:
        hT = k.sb(c, f"pe_hT{l}", [P, DC, S])
        norm_transpose(k, f"pe_n{l}", x, TT, k.col(f"norm_ffn{l}"), hT)
        with ExitStack() as c2:
            vals = k.sb(c2, f"pe_vals{l}", [P, TT, HK])
            key1 = k.sb(c2, f"pe_key1{l}", [P, TT, HK])
            key2 = k.sb(c2, f"pe_key2{l}", [P, TT, HK])
            rows = k.sb(c2, f"pe_rows{l}", [P, 3, S])
            route(k, l, hT, vals, key1, key2)
            gate_softmax(k, l, vals, key1, key2, rows)
            spread_gates(k, l, rows, gmat)
        experts(k, l, hT, x, gmat)


def build(nc, dram, out, stop=99):
    with ExitStack() as ctx:
        k = Chip(nc, ctx)
        k.dram = dram
        k.params = k.sb(ctx, "params_sb", [P, NCOLS])
        x = k.sb(ctx, "x_sb", [P, TT, D])
        gmat = nc.dram_tensor("gate_matrix", (P, NTB, NK, TB), F32, kind="Internal").ap()
        load(k, "params", [(k.params[:], dram["params"]), (x[:], dram["x"].rearrange("(t p) d -> p t d", p=P))])

        def finish():
            stored = k.sig("out_stored")
            with nc.Block() as block:
                @block.sync
                def _(sp):
                    sp.dma_start(out.rearrange("(t p) d -> p t d", p=P), x[:]).then_inc(stored.sem, 16)
                    sp.wait_ge(stored.sem, stored.base + 16)

        with ExitStack() as c:
            mixT = k.sb(c, "mixT0", [P, DC, S])
            proj = k.sb(c, "proj0", [P, 2 * LRU_CH + MEM_CH, S])
            with ExitStack() as c2:
                hT = k.sb(c2, "hT0", [P, DC, S])
                norm_transpose(k, "n0", x, TT, k.col("norm_mix0"), hT)
                project(k, "p0", dram["a_w_in"], 2 * LRU_CH + MEM_CH, hT[:], S, proj)
            recurrent(k, proj, mixT)
            memory_attention(k, 0, proj[:, 2 * LRU_CH:, :], mixT)
            out_project(k, 0, mixT, x)
        if stop >= 2:
            peer(k, 0, x, gmat)
        if stop >= 3:
            with ExitStack() as c:
                cos = k.sb(c, "rope_cos", [P, S])
                sin = k.sb(c, "rope_sin", [P, S])
                rope_tables(k, cos, sin)
                kc = k.sb(c, "kc", [P, 1, CMPW])
                vc = k.sb(c, "vc", [CMPW, 2 * HD])
                keysT = k.sb(c, "keysT", [P, 6, S])
                vals = k.sb(c, "vals", [P, TT, 4 * HD])
                with ExitStack() as c2:
                    hT = k.sb(c2, "hTkv", [P, DC, S])
                    norm_transpose(k, "nkv", x, TT, k.col("kv_norm"), hT)
                    project(k, "pkv", dram["w_keys"], 6, hT[:], S, keysT)
                    natural(k, "pv", dram["w_vals"], 4 * HD, hT, TT, vals)
                head_norm(k, "hk", keysT[:, 4:6, :], 2, S, [k.col("k_gain", 1, 1), k.col("k_gain", 2, 1)],
                          [(cos[:], sin[:])] * 2)
                compress(k, keysT, cos, sin, kc, vc)
                mixT = k.sb(c, "mixT1", [P, DC, S])
                proj = k.sb(c, "proj1", [P, DC, S])
                gates = k.sb(c, "gates", [P, TT, 36])
                with ExitStack() as c2:
                    hT = k.sb(c2, "hT1", [P, DC, S])
                    norm_transpose(k, "n1", x, TT, k.col("norm_mix1"), hT)
                    project(k, "p1", dram["b_w_in"], DC, hT[:], S, proj)
                    natural(k, "pg", dram["w_gates"], 36, hT, TT, gates)
                nsa_gates(k, gates)
                head_norm(k, "hq", proj[:, 0:LRU_CH, :], LRU_CH, S, [k.col("q_gain")] * LRU_CH, [(cos[:], sin[:])] * LRU_CH)
                with ExitStack() as c2:
                    q_now = k.sb(c2, "q_now", [P, S])
                    gate_now = k.sb(c2, "gate_now", [P, TT, 6])
                    units = []
                    for t in range(TT):
                        for half in range(2):
                            gate = lambda b: gate_now[:, t, 3 * half + b:3 * half + b + 1]
                            cols = slice(half * HD, (half + 1) * HD)
                            units.append((half, t, kc[:, 0, :], CMPW, k.col("cmpmask", t * CMPW, CMPW), gate(0),
                                          (lambda j, cols=cols: vc[:, cols])))
                            for b in range(2):
                                at = slice(2 * b * HD + half * HD, 2 * b * HD + (half + 1) * HD)
                                units.append((half, t, keysT[:, 4 + b, :], (t + 1) * P, k.col("causal"), gate(1 + b),
                                              (lambda j, at=at: vals[:, j, at])))
                    staged = [
                        (q_now[:], lambda r: proj[:, bass.ds(r, 1), :].rearrange("p a n -> p (a n)")),
                        (gate_now[:], lambda r: gates[:, :, bass.ds(r * 6, 6)]),
                    ]
                    attention(k, "nsa", LRU_CH, staged, units,
                              lambda r, t: mixT[:, bass.ds(r, 1), t * P:(t + 1) * P].rearrange("p a n -> p (a n)"))
                memory_attention(k, 1, proj[:, LRU_CH:, :], mixT)
                out_project(k, 1, mixT, x)
        if stop >= 4:
            peer(k, 1, x, gmat)
        finish()


def chunks_T(w):
    return np.ascontiguousarray(w.reshape(DC, P, -1, P).transpose(2, 1, 0, 3))


def rows_first(w):
    return np.ascontiguousarray(w.reshape(DC, P, -1).transpose(1, 0, 2))


def shape_constants():
    rot = np.zeros((P, P), np.float32)
    mean = np.zeros((P, P), np.float32)
    for h in (0, HD):
        mean[h:h + HD, h:h + HD] = 1.0 / HD
        for i in range(ROPE_HALF):
            rot[h + ROPE_HALF + i, h + i] = -1.0
            rot[h + i, h + ROPE_HALF + i] = 1.0
    freq = np.zeros((P, 1), np.float32)
    f = np.float32(THETA) ** (-np.arange(ROPE_HALF, dtype=np.float32) / np.float32(ROPE_HALF))
    for h in (0, HD):
        freq[h:h + ROPE_HALF, 0] = f
        freq[h + ROPE_HALF:h + 2 * ROPE_HALF, 0] = f
    t = np.arange(P)
    causal = np.where(t[None, :] <= t[:, None], 0.0, NEG).astype(np.float32)
    end = np.arange(CMPW) * CMP_STRIDE + CMP_LEN - 1
    tok = np.arange(S).reshape(TT, P)
    cmp = np.where((end[None, None] <= tok[:, :, None]) & (np.arange(CMPW) < N_CMP)[None, None], 0.0, NEG)
    return {
        "ident": np.eye(P, dtype=np.float32), "rot": rot, "headmean": mean, "causal": causal,
        "cmpmask": cmp.transpose(1, 0, 2).reshape(P, TT * CMPW).astype(np.float32),
        "iota": np.tile(np.arange(P, dtype=np.float32), (P, 1)), "freq": freq,
        "rowvalid": (t >= CMP_LEN - 1).astype(np.float32)[:, None],
    }


def laid_out(i):
    by_channel = lambda v: v.reshape(-1, P).T
    twice = lambda v: np.concatenate([v, v])[:, None]
    cols = shape_constants()
    for l in range(LAYERS):
        cols[f"norm_mix{l}"] = by_channel(i["norm_mix"][l])
        cols[f"norm_ffn{l}"] = by_channel(i["norm_ffn"][l])
        cols[f"norm_mem{l}"] = by_channel(i["norm_mem"][l])
        cols[f"mq_gain{l}"] = twice(i["mem_q_gain"][l])
        cols[f"mk_gain{l}"] = twice(i["mem_k_gain"][l])
    cols["kv_norm"] = by_channel(i["kv_norm"])
    cols["conv_w"] = i["a_conv_w"][0].T.reshape(LRU_CH, P, 4).transpose(1, 0, 2).reshape(P, -1)
    cols["conv_b"] = by_channel(i["a_conv_b"][0])
    cols["gate_b"] = np.concatenate([by_channel(i["a_gate_b"][0, g]) for g in range(2)], axis=1)
    cols["lam"] = by_channel(i["a_lambda"][0])
    cols["q_gain"] = twice(i["b_q_gain"][0])
    cols["k_gain"] = np.concatenate([twice(i["k_gain_shared"][b]) for b in range(3)], axis=1)
    cols["cmp_b1"] = np.concatenate([by_channel(i["cmp_b1"][j]) for j in range(2)], axis=1)
    heads = [h for c in range(LRU_CH) for h in (c, c + LRU_CH)]
    cols["nsa_gate_b"] = np.tile(i["b_gate_b"][0].reshape(12, 3)[heads].reshape(1, 36), (P, 1))
    cols["cmp_pos"] = i["cmp_pos"].reshape(2, CMP_LEN // 2, 2, HD).transpose(2, 3, 0, 1).reshape(P, -1)
    a = {"params": np.ascontiguousarray(np.concatenate([cols[n].reshape(P, w) for n, w in COLS], axis=1))}
    a["x"], a["mem"], a["positions"] = i["x"][0], i["mem"][0], i["positions"]
    a["a_w_in"] = chunks_T(i["a_w_in"][0])
    gw = np.zeros((P, LRU_CH, 2, P), np.float32)
    for c in range(LRU_CH):
        for g in range(2):
            for h in range(2):
                gw[h * HD:(h + 1) * HD, c, g, h * HD:(h + 1) * HD] = i["a_gate_w"][0, g, 2 * c + h]
    a["gate_w"] = gw
    w = i["b_w_in"][0]
    q = w[:, :768].reshape(D, 12, HD)[:, heads].reshape(D, 768)
    a["b_w_in"] = chunks_T(np.concatenate([q, w[:, 804:]], axis=1))
    a["w_gates"] = rows_first(w[:, 768:804].reshape(D, 12, 3)[:, heads].reshape(D, 36))
    kv = i["w_kv_shared"].reshape(D, 3, 2, 2, HD)
    dup = lambda m: np.concatenate([m, m], axis=1)
    a["w_keys"] = chunks_T(np.concatenate(
        [dup(kv[:, 0, j, g]) for j in range(2) for g in range(2)] + [kv[:, b, 0].reshape(D, P) for b in (1, 2)], axis=1))
    a["w_vals"] = rows_first(np.concatenate([kv[:, b, 1].reshape(D, P) for b in (1, 2)], axis=1))
    a["cmp_w1"], a["cmp_w2"] = i["cmp_w1"], i["cmp_w2"]
    for l in range(LAYERS):
        a[f"w_mem_k{l}"] = chunks_T(i["w_mem_kv"][l][:, :256])
        a[f"w_mem_v{l}"] = rows_first(i["w_mem_kv"][l][:, 256:])
        w = i["w_out"][l]
        if l:
            w = np.concatenate([w[:768].reshape(12, HD, D)[heads].reshape(768, D), w[768:]], axis=0)
        a[f"w_out{l}"] = w
        a[f"peer_wq{l}"] = chunks_T(i["peer_wq"][l])
        a[f"subkeys{l}"] = i["peer_subkeys"][l].reshape(2 * PH, NK, P).transpose(0, 2, 1)
        a[f"uT{l}"] = i["peer_u"][l].reshape(NK, P, DC, P).transpose(0, 3, 2, 1)
        a[f"v{l}"] = i["peer_v"][l]
    return {n: np.ascontiguousarray(v) for n, v in a.items()}


STOP = 99


def kernel(**inputs):
    import concourse.bacc as bacc
    from concourse.bass_utils import run_bass_kernel_spmd as run

    nc = bacc.Bacc("TRN2", target_bir_lowering=False, num_devices=1)
    arrays = laid_out({n: np.asarray(v) for n, v in inputs.items()})
    dram = {n: nc.dram_tensor("in_" + n, v.shape, mybir.dt.from_np(v.dtype), kind="ExternalInput").ap()
            for n, v in arrays.items()}
    out = nc.dram_tensor("out", (S, D), F32, kind="ExternalOutput").ap()
    build(nc, dram, out, STOP)
    r = run(nc, [{"in_" + n: v for n, v in arrays.items()}], core_ids=[0])
    return r.results[0]["out"][None]
```

```python
from contextlib import ExitStack

import numpy as np

import concourse.bass as bass
from concourse import mybir

F32 = mybir.dt.float32
F32R = mybir.dt.float32r
I32 = mybir.dt.int32
U32 = mybir.dt.uint32
ALU = mybir.AluOpType
ACT = mybir.ActivationFunctionType
AX = mybir.AxisListType

P = 128
D = 1024
S = 512
DC = D // P
TT = S // P
HD = 64
EPS = 1e-6
NEG = -1e30
LRU_CH = 6
MEM_CH = 2
MEMLEN = 256
MT = MEMLEN // P
LAYERS = 2
ROPE_HALF = 8
THETA = 500000.0
N_CMP = 31
CMPW = 32
CMP_STRIDE = 16
CMP_LEN = 32
HID = 256
SCALE = HD ** -0.5
PH = 8
TOPK = 16
HK = PH * TOPK
NK = 128
TB = 64
NTB = S // TB
GT = 2
NG = NK // GT
EARLY = GT * (PH + NTB)
EG = EARLY // GT

COLS = [
    ("norm_mix0", 8), ("norm_mix1", 8), ("norm_ffn0", 8), ("norm_ffn1", 8), ("norm_mem0", 8), ("norm_mem1", 8),
    ("kv_norm", 8), ("conv_w", 4 * LRU_CH), ("conv_b", LRU_CH), ("gate_b", 2 * LRU_CH), ("lam", LRU_CH),
    ("mq_gain0", 1), ("mq_gain1", 1), ("mk_gain0", 1), ("mk_gain1", 1), ("q_gain", 1), ("k_gain", 3),
    ("cmp_b1", 4), ("nsa_gate_b", 36), ("cmp_pos", 32),
    ("freq", 1), ("rowvalid", 1), ("ident", P), ("rot", P), ("headmean", P), ("causal", P), ("cmpmask", TT * CMPW),
    ("iota", P),
]
OFF = {}
_at = 0
for _n, _w in COLS:
    OFF[_n] = (_at, _w)
    _at += _w
NCOLS = _at


class Signal:

    def __init__(self, sem, credit=0):
        self.sem, self.base, self.credit = sem, 0, credit
        self.given = False

    def free(self, n):
        return self.base + n + 1

    def done(self, n):
        return self.base + self.credit + n + 1

    def passed(self, n):
        self.base += n

    def give(self, eng):
        if not self.given:
            self.given = True
            eng.sem_inc(self.sem, self.credit)


class Chip:

    def __init__(self, nc, ctx):
        self.nc, self.ctx, self.signals = nc, ctx, {}

    def sb(self, ctx, name, shape, dt=F32):
        return ctx.enter_context(self.nc.sbuf_tensor(name, shape, dt))

    def ps(self, ctx, name, shape, dt=F32):
        return ctx.enter_context(self.nc.psum_tensor(name, shape, dt))

    def sig(self, name, credit=0):
        if name not in self.signals:
            self.signals[name] = Signal(self.ctx.enter_context(self.nc.semaphore(name)), credit)
        return self.signals[name]

    def col(self, name, a=0, n=None):
        at, w = OFF[name]
        n = w - a if n is None else n
        return self.params[:, at + a:at + a + n]


def bc(ap, shape):
    return ap.to_broadcast(shape)


def load(k, name, pairs):
    nc = k.nc
    loaded = k.sig("loaded")
    with nc.Block() as block:
        @block.sync
        def _(sp):
            for dst, src in pairs:
                sp.dma_start(dst, src).then_inc(loaded.sem, 16)
            sp.wait_ge(loaded.sem, loaded.base + 16 * len(pairs))
    loaded.passed(16 * len(pairs))


def norm_transpose(k, name, src, nt, gain, out):
    nc = k.nc
    squares, mean_ready, std_ready = k.sig("nt_squares"), k.sig("nt_mean"), k.sig("nt_std")
    scaled, turned, stored = k.sig("nt_scaled"), k.sig("nt_turned"), k.sig("nt_stored", 4)
    with ExitStack() as c:
        xn = k.sb(c, name + "_xn", [P, nt, D])
        dump = k.sb(c, name + "_dump", [P, D])
        ssq = k.sb(c, name + "_ssq", [P, nt])
        std = k.sb(c, name + "_std", [P, nt])
        rstd = k.sb(c, name + "_rstd", [P, nt])
        ps = k.ps(c, name + "_ps", [P, 4, 4, P])
        block = c.enter_context(nc.Block())
        ident = k.col("ident")

        @block.scalar
        def _(act):
            for t in range(nt):
                act.activation(dump[:], src[:, t, :], ACT.Square, accum_out=ssq[:, t:t + 1]).then_inc(squares.sem, 1)
                act.drain()
            act.wait_ge(mean_ready.sem, mean_ready.done(0))
            act.activation(std[:], ssq[:], ACT.Sqrt).then_inc(std_ready.sem, 1)

        @block.vector
        def _(dve):
            stored.give(dve)
            dve.wait_ge(squares.sem, squares.done(nt - 1))
            dve.tensor_scalar(ssq[:], ssq[:], 1.0 / D, EPS, ALU.mult, ALU.add).then_inc(mean_ready.sem, 1)
            dve.wait_ge(std_ready.sem, std_ready.done(0))
            dve.reciprocal(rstd[:], std[:])
            dve.drain()
            for t in range(nt):
                dve.tensor_scalar(xn[:, t, :], src[:, t, :], rstd[:, t:t + 1], None, ALU.mult).then_inc(scaled.sem, 1)
            for n in range(2 * nt):
                t, h = n // 2, n % 2
                dve.wait_ge(turned.sem, turned.done(n))
                dve.tensor_tensor(out[:, 4 * h:4 * h + 4, t * P:(t + 1) * P], ps[:, n % 4, :, :],
                                  bc(gain[:, 4 * h:4 * h + 4].unsqueeze(2), [P, 4, P]), ALU.mult).then_inc(stored.sem, 1)

        @block.tensor
        def _(pe):
            for n in range(2 * nt):
                t, h = n // 2, n % 2
                pe.wait_ge(scaled.sem, scaled.done(t))
                pe.wait_ge(stored.sem, stored.free(n))
                for q in range(4):
                    ch = 4 * h + q
                    last = pe.transpose(ps[:, n % 4, q, :], xn[:, t, ch * P:(ch + 1) * P], ident)
                last.then_inc(turned.sem, 1)
    squares.passed(nt)
    mean_ready.passed(1)
    std_ready.passed(1)
    scaled.passed(nt)
    turned.passed(2 * nt)
    stored.passed(2 * nt)


def project(k, name, w, n, rhs, width, out):
    nc = k.nc
    loaded = [k.sig("pj_loaded0"), k.sig("pj_loaded1")]
    product, stored = k.sig("pj_product", 2), k.sig("pj_stored", 2)
    rounds = n // 2
    with ExitStack() as c:
        wb = k.sb(c, name + "_w", [P, 2, DC, P])
        ps = k.ps(c, name + "_ps", [P, 2, 512])
        block = c.enter_context(nc.Block())

        @block.sync
        def _(sp):
            with sp.Fori(0, rounds) as r:
                for b in range(2):
                    sp.wait_ge(product.sem, r * 2 + product.free(b))
                    sp.dma_start(wb[:, b, :, :], w[bass.ds(r * 2 + b, 1), :, :, :].rearrange("a p c m -> p (a c) m")
                                 ).then_inc(loaded[b].sem, 16)

        @block.tensor
        def _(pe):
            product.give(pe)
            with pe.Fori(0, rounds) as r:
                for b in range(2):
                    pe.wait_ge(loaded[b].sem, r * 16 + loaded[b].base + 16)
                    pe.wait_ge(stored.sem, r * 2 + stored.free(b))
                    for dc in range(DC):
                        last = pe.matmul(ps[:, b, 0:width], wb[:, b, dc, :], rhs[:, dc, :],
                                         start=(dc == 0), stop=(dc == DC - 1))
                    last.then_inc(product.sem, 1)

        @block.scalar
        def _(act):
            stored.give(act)
            with act.Fori(0, rounds) as r:
                for b in range(2):
                    act.wait_ge(product.sem, r * 2 + product.done(b))
                    act.activation(out[:, bass.ds(r * 2 + b, 1), :].rearrange("p a n -> p (a n)"), ps[:, b, 0:width],
                                   ACT.Copy).then_inc(stored.sem, 1)
    for s in loaded:
        s.passed(16 * rounds)
    product.passed(n)
    stored.passed(n)


def natural(k, name, w, width, lhs, nt, out):
    nc = k.nc
    loaded, product = k.sig("na_loaded"), k.sig("na_product")
    with ExitStack() as c:
        wb = k.sb(c, name + "_w", [P, DC, width])
        ps = k.ps(c, name + "_ps", [P, nt, 512])
        block = c.enter_context(nc.Block())

        @block.sync
        def _(sp):
            sp.dma_start(wb[:], w).then_inc(loaded.sem, 16)

        @block.tensor
        def _(pe):
            pe.wait_ge(loaded.sem, loaded.base + 16)
            for t in range(nt):
                for dc in range(DC):
                    last = pe.matmul(ps[:, t, 0:width], lhs[:, dc, t * P:(t + 1) * P], wb[:, dc, :],
                                     start=(dc == 0), stop=(dc == DC - 1))
                last.then_inc(product.sem, 1)

        @block.scalar
        def _(act):
            for t in range(nt):
                act.wait_ge(product.sem, product.done(t))
                act.activation(out[:, t, :], ps[:, t, 0:width], ACT.Copy)
    loaded.passed(16)
    product.passed(nt)


def head_norm(k, name, src, n, width, gains, rope=None):
    nc = k.nc
    squared, mean, eps_added, root, normed = (k.sig(x) for x in ("hn_squared", "hn_mean", "hn_eps", "hn_root", "hn_normed"))
    rotated, turned = k.sig("hn_rotated"), k.sig("hn_turned", 2)
    roped = [i for i in range(n) if rope and rope[i]]
    with ExitStack() as c:
        sq = k.sb(c, name + "_sq", [P, n, width])
        t1 = k.sb(c, name + "_t1", [P, width])
        t2 = k.sb(c, name + "_t2", [P, width])
        ps = k.ps(c, name + "_ps", [P, 8, 512])
        block = c.enter_context(nc.Block())

        @block.scalar
        def _(act):
            act.activation(sq[:], src, ACT.Square).then_inc(squared.sem, 1)
            act.wait_ge(eps_added.sem, eps_added.done(0))
            act.activation(sq[:], sq[:], ACT.Sqrt).then_inc(root.sem, 1)

        @block.tensor
        def _(pe):
            pe.wait_ge(squared.sem, squared.done(0))
            for i in range(n):
                last = pe.matmul(ps[:, i, 0:width], k.col("headmean"), sq[:, i, :], start=True, stop=True)
            last.then_inc(mean.sem, 1)
            for m, i in enumerate(roped):
                pe.wait_ge(normed.sem, normed.done(i))
                pe.wait_ge(turned.sem, turned.free(m))
                pe.matmul(ps[:, m % 2, 0:width], k.col("rot"), src[:, i, :], start=True, stop=True).then_inc(rotated.sem, 1)

        @block.vector
        def _(dve):
            turned.give(dve)
            dve.wait_ge(mean.sem, mean.done(0))
            dve.tensor_scalar(sq[:], ps[:, 0:n, 0:width], EPS, None, ALU.add).then_inc(eps_added.sem, 1)
            dve.wait_ge(root.sem, root.done(0))
            dve.reciprocal(sq[:], sq[:])
            dve.drain()
            for i in range(n):
                dve.scalar_tensor_tensor(out=src[:, i, :], in0=src[:, i, :], scalar=gains[i], in1=sq[:, i, :],
                                         op0=ALU.mult, op1=ALU.mult).then_inc(normed.sem, 1)
            for m, i in enumerate(roped):
                cos, sin = rope[i]
                dve.wait_ge(rotated.sem, rotated.done(m))
                dve.tensor_tensor(t1[:], ps[:, m % 2, 0:width], sin, ALU.mult).then_inc(turned.sem, 1)
                dve.tensor_tensor(t2[:], src[:, i, :], cos, ALU.mult)
                dve.drain()
                dve.tensor_tensor(src[:, i, :], t1[:], t2[:], ALU.add)
                dve.drain()
    for s in (squared, mean, eps_added, root):
        s.passed(1)
    normed.passed(n)
    rotated.passed(len(roped))
    turned.passed(len(roped))


def rope_tables(k, cos, sin):
    nc = k.nc
    loaded, reduced = k.sig("rt_loaded"), k.sig("rt_reduced")
    two_pi = 2.0 * np.pi
    part1 = float(np.float32(6.28125))
    part2 = float(np.float32(np.float32((two_pi - part1) * 2 ** 20).astype(np.int32) >> 2 << 2) / np.float32(2 ** 20))
    part3 = float(np.float32(two_pi - part1 - part2))
    magic = 1.5 * 2.0 ** 23
    pi = float(np.nextafter(np.float32(np.pi), np.float32(0)))
    with ExitStack() as c:
        pos = k.sb(c, "rt_pos", [P, S], I32)
        ang = k.sb(c, "rt_ang", [P, S])
        turns = k.sb(c, "rt_turns", [P, S])
        block = c.enter_context(nc.Block())

        @block.sync
        def _(sp):
            sp.dma_start(pos[:], bc(k.dram["positions"].rearrange("(a n) -> a n", a=1), [P, S])).then_inc(loaded.sem, 16)

        @block.vector
        def _(dve):
            dve.wait_ge(loaded.sem, loaded.base + 16)
            dve.tensor_copy(ang[:], pos[:])
            dve.drain()
            dve.tensor_scalar(ang[:], ang[:], k.col("freq"), None, ALU.mult)
            dve.drain()
            for out, quarter in ((sin, 0.0), (cos, 0.25)):
                dve.tensor_scalar(turns[:], ang[:], 1.0 / two_pi, quarter, ALU.mult, ALU.add)
                dve.drain()
                dve.tensor_scalar(turns[:], turns[:], magic, None, ALU.add)
                dve.drain()
                dve.tensor_scalar(turns[:], turns[:], magic, None, ALU.subtract)
                dve.drain()
                dve.scalar_tensor_tensor(out=out[:], in0=turns[:], scalar=-part1, in1=ang[:], op0=ALU.mult, op1=ALU.add)
                dve.drain()
                dve.scalar_tensor_tensor(out=out[:], in0=turns[:], scalar=-part2, in1=out[:], op0=ALU.mult, op1=ALU.add)
                dve.drain()
                dve.scalar_tensor_tensor(out=out[:], in0=turns[:], scalar=-part3, in1=out[:], op0=ALU.mult, op1=ALU.add)
                dve.drain()
                if quarter:
                    dve.tensor_scalar(out[:], out[:], float(np.float32(np.pi / 2)), None, ALU.add)
                    dve.drain()
                dve.tensor_scalar(out[:], out[:], pi, -pi, ALU.min, ALU.max).then_inc(reduced.sem, 1)
                dve.drain()

        @block.scalar
        def _(act):
            for n, out in enumerate((sin, cos)):
                act.wait_ge(reduced.sem, reduced.done(n))
                act.activation(out[:], out[:], ACT.Sin)
    loaded.passed(16)
    reduced.passed(2)


def recurrent(k, proj, mixT):
    nc = k.nc
    gates_loaded, convolved, gated, opened = (k.sig(x) for x in ("rc_gates_loaded", "rc_conv", "rc_gated", "rc_opened"))
    decay_ready, exps, left_ready, rooted, gelu_ready = (k.sig(x) for x in ("rc_decay", "rc_exps", "rc_left", "rc_root", "rc_gelu"))
    freed = k.sig("rc_freed", 2)
    y_exp, y_ready = k.sig("rc_yexp"), k.sig("rc_y")
    n = LRU_CH
    with ExitStack() as c:
        gw = k.sb(c, "rc_gw", [P, n, 2, P])
        xc = k.sb(c, "rc_xc", [P, n, S])
        rec = k.sb(c, "rc_rec", [P, n, S])
        inp = k.sb(c, "rc_inp", [P, n, S])
        dec = k.sb(c, "rc_dec", [P, n, S])
        tnh = k.sb(c, "rc_tnh", [P, n, S])
        sp_ = k.sb(c, "rc_softplus", [P, 4, n])
        ps = k.ps(c, "rc_ps", [P, 2, 2, 512])
        block = c.enter_context(nc.Block())
        lam = k.col("lam")

        @block.sync
        def _(sp):
            sp.dma_start(gw[:], k.dram["gate_w"]).then_inc(gates_loaded.sem, 16)

        @block.tensor
        def _(pe):
            pe.wait_ge(gates_loaded.sem, gates_loaded.base + 16)
            for i in range(n):
                pe.wait_ge(convolved.sem, convolved.done(i))
                pe.wait_ge(freed.sem, freed.free(i))
                for g in range(2):
                    last = pe.matmul(ps[:, i % 2, g, :], gw[:, i, g, :], xc[:, i, :], start=True, stop=True)
                last.then_inc(gated.sem, 1)

        @block.scalar
        def _(act):
            freed.give(act)
            act.activation(sp_[:, 0, :], lam, ACT.Abs)
            act.drain()
            act.activation(sp_[:, 1, :], sp_[:, 0, :], ACT.Exp, scale=-1.0).then_inc(y_exp.sem, 1)
            for i in range(n):
                act.wait_ge(gated.sem, gated.done(i))
                act.activation(rec[:, i, :], ps[:, i % 2, 0, :], ACT.Sigmoid, bias=k.col("gate_b", i, 1)).then_inc(opened.sem, 1)
                act.activation(inp[:, i, :], ps[:, i % 2, 1, :], ACT.Sigmoid, bias=k.col("gate_b", n + i, 1)).then_inc(freed.sem, 1)
            act.wait_ge(decay_ready.sem, decay_ready.done(0))
            act.activation(dec[:], rec[:], ACT.Exp, scale=-1.0).then_inc(exps.sem, 1)
            act.activation(tnh[:], rec[:], ACT.Tanh).then_inc(exps.sem, 1)
            act.activation(proj[:, n:2 * n, :], proj[:, n:2 * n, :], ACT.Gelu_apprx_tanh).then_inc(gelu_ready.sem, 1)
            act.wait_ge(left_ready.sem, left_ready.done(0))
            act.activation(rec[:], rec[:], ACT.Sqrt).then_inc(rooted.sem, 1)

        @block.vector
        def _(dve):
            for i in range(n):
                dve.tensor_scalar(xc[:, i, :], proj[:, i, :], k.col("conv_w", 4 * i + 3, 1), k.col("conv_b", i, 1),
                                  ALU.mult, ALU.add)
                for s in (1, 2, 3):
                    dve.drain()
                    last = dve.scalar_tensor_tensor(out=xc[:, i, s:S], in0=proj[:, i, 0:S - s],
                                                    scalar=k.col("conv_w", 4 * i + 3 - s, 1), in1=xc[:, i, s:S],
                                                    op0=ALU.mult, op1=ALU.add)
                last.then_inc(convolved.sem, 1)
            y, s_, s2, acc = (sp_[:, j, :] for j in (1, 2, 0, 3))
            dve.wait_ge(y_exp.sem, y_exp.done(0))
            dve.tensor_scalar(s_, y, 2.0, None, ALU.add)
            dve.drain()
            dve.reciprocal(s_, s_)
            dve.drain()
            dve.tensor_tensor(s_, s_, y, ALU.mult)
            dve.drain()
            dve.tensor_tensor(s2, s_, s_, ALU.mult)
            dve.memset(acc, 1.0 / 19)
            dve.drain()
            for m in (17, 15, 13, 11, 9, 7, 5, 3, 1):
                dve.tensor_tensor(acc, acc, s2, ALU.mult)
                dve.drain()
                dve.tensor_scalar(acc, acc, 1.0 / m, None, ALU.add)
                dve.drain()
            dve.scalar_tensor_tensor(out=acc, in0=acc, scalar=2.0, in1=s_, op0=ALU.mult, op1=ALU.mult)
            dve.tensor_scalar(s2, lam, -1.0, 0.0, ALU.mult, ALU.max)
            dve.drain()
            dve.tensor_tensor(acc, acc, s2, ALU.add)
            dve.drain()
            dve.tensor_scalar(acc, acc, 8.0, None, ALU.mult)
            dve.drain()
            for i in range(n):
                dve.wait_ge(opened.sem, opened.done(i))
                last = dve.tensor_scalar(rec[:, i, :], rec[:, i, :], sp_[:, 3, i:i + 1], None, ALU.mult)
            last.then_inc(decay_ready.sem, 1)
            dve.wait_ge(freed.sem, freed.done(n - 1))
            dve.tensor_tensor(inp[:], inp[:], xc[:], ALU.mult)
            dve.wait_ge(exps.sem, exps.done(1))
            dve.drain()
            dve.tensor_tensor(xc[:], dec[:], dec[:], ALU.mult)
            dve.drain()
            dve.scalar_tensor_tensor(out=xc[:], in0=xc[:], scalar=1.0, in1=tnh[:], op0=ALU.add, op1=ALU.mult)
            dve.drain()
            dve.tensor_scalar(rec[:], xc[:], 1e-34, None, ALU.max).then_inc(left_ready.sem, 1)
            dve.wait_ge(rooted.sem, rooted.done(0))
            dve.tensor_tensor(inp[:], inp[:], rec[:], ALU.mult)
            dve.drain()
            for i in range(n):
                dve.tensor_tensor_scan(tnh[:, i, :], dec[:, i, :], inp[:, i, :], 0.0, ALU.mult, ALU.add)
            dve.wait_ge(gelu_ready.sem, gelu_ready.done(0))
            dve.drain()
            dve.tensor_tensor(mixT[:, 0:n, :], tnh[:], proj[:, n:2 * n, :], ALU.mult)
    gates_loaded.passed(16)
    for s in (convolved, gated, opened, freed):
        s.passed(n)
    for s in (decay_ready, left_ready, rooted, gelu_ready, y_exp):
        s.passed(1)
    exps.passed(2)


def attention(k, name, rounds, staged, units, o_out):
    nc = k.nc
    U = len(units)
    per_tile = U // TT
    R = 3
    copied, scored, maxed = k.sig("at_copied"), k.sig("at_scored"), k.sig("at_maxed")
    expd, scaled = k.sig("at_exp", R), k.sig("at_scaled")
    turned, stored = k.sig("at_turned", R), k.sig("at_stored", R)
    summed, out_done = k.sig("at_summed", R), k.sig("at_out", 2)
    copied_per = len(staged)
    with ExitStack() as c:
        prob = k.sb(c, name + "_p", [P, R, 512])
        probT = k.sb(c, name + "_pt", [P, R, 512])
        mx = k.sb(c, name + "_mx", [P, 4])
        nb = k.sb(c, name + "_nb", [P, 4])
        sm = k.sb(c, name + "_sm", [P, 4])
        rs = k.sb(c, name + "_rs", [P, 4])
        psS = k.ps(c, name + "_pss", [P, R, 512])
        psT = k.ps(c, name + "_pst", [P, R, 512])
        psO = k.ps(c, name + "_pso", [P, 2, 512])
        block = c.enter_context(nc.Block())

        @block.gpsimd
        def _(pool):
            with pool.Fori(0, rounds) as r:
                pool.wait_ge(out_done.sem, r * TT + out_done.base + 2)
                for dst, src in staged:
                    pool.tensor_copy(dst, src(r)).then_inc(copied.sem, 1)

        @block.tensor
        def _(pe):
            turned.give(pe)
            summed.give(pe)
            with pe.Fori(0, rounds) as r:
                pe.wait_ge(copied.sem, r * copied_per + copied.done(copied_per - 1))
                for step in range(U + 3):
                    if step < U:
                        half, t, keys, width, _, _, _ = units[step]
                        b = HD * half
                        pe.wait_ge(expd.sem, r * U + expd.free(step))
                        q = staged[0][0]
                        pe.matmul(psS[:, step % R, 0:width], q[b:b + HD, t * P:(t + 1) * P], keys[b:b + HD, 0:width],
                                  start=True, stop=True).then_inc(scored.sem, 1)
                    u = step - 2
                    if 0 <= u < U:
                        width = units[u][3]
                        pe.wait_ge(scaled.sem, r * U + scaled.done(u))
                        pe.wait_ge(stored.sem, r * U + stored.free(u))
                        for j in range(0, width, P):
                            w = min(P, width - j)
                            last = pe.transpose(psT[0:w, u % R, j:j + P], prob[:, u % R, j:j + w], k.col("ident"))
                        last.then_inc(turned.sem, 1)
                    u = step - 3
                    if 0 <= u < U:
                        half, t, _, width, _, _, values = units[u]
                        b = HD * half
                        of_head = [m for m in range(U) if units[m][0] == half and units[m][1] == t]
                        pe.wait_ge(stored.sem, r * U + stored.done(u))
                        if u % per_tile == 0:
                            pe.wait_ge(out_done.sem, r * TT + out_done.free(t))
                        blocks = range(0, width, P)
                        for j in blocks:
                            w = min(P, width - j)
                            last = pe.matmul(psO[b:b + HD, t % 2, 0:P], values(j // P), probT[0:w, u % R, j:j + P],
                                             start=(u == of_head[0] and j == 0),
                                             stop=(u == of_head[-1] and j == blocks[-1]))
                        last.then_inc(summed.sem, 1)

        @block.vector
        def _(dve):
            with dve.Fori(0, rounds) as r:
                for step in range(U + 1):
                    if step < U:
                        _, _, _, width, mask, _, _ = units[step]
                        dve.wait_ge(scored.sem, r * U + scored.done(step))
                        if mask is not None:
                            mw = mask.shape[1]
                            part = psS[:, step % R, width - mw:width]
                            dve.tensor_tensor(part, part, mask, ALU.add)
                            dve.drain()
                        dve.tensor_reduce(mx[:, step % 4:step % 4 + 1], psS[:, step % R, 0:width], AX.X, ALU.max)
                        dve.drain()
                        dve.tensor_scalar(nb[:, step % 4:step % 4 + 1], mx[:, step % 4:step % 4 + 1], -SCALE, None,
                                          ALU.mult).then_inc(maxed.sem, 1)
                    u = step - 1
                    if 0 <= u < U:
                        _, _, _, width, _, gate, _ = units[u]
                        dve.wait_ge(expd.sem, r * U + expd.done(u))
                        dve.reciprocal(rs[:, u % 4:u % 4 + 1], sm[:, u % 4:u % 4 + 1])
                        dve.drain()
                        if gate is not None and u == 0:
                            dve.wait_ge(copied.sem, r * copied_per + copied.done(copied_per - 1))
                        if gate is None:
                            dve.tensor_scalar(prob[:, u % R, 0:width], prob[:, u % R, 0:width], rs[:, u % 4:u % 4 + 1],
                                              None, ALU.mult).then_inc(scaled.sem, 1)
                        else:
                            dve.tensor_scalar(prob[:, u % R, 0:width], prob[:, u % R, 0:width], rs[:, u % 4:u % 4 + 1],
                                              gate, ALU.mult, ALU.mult).then_inc(scaled.sem, 1)

        @block.scalar
        def _(act):
            expd.give(act)
            stored.give(act)
            out_done.give(act)
            with act.Fori(0, rounds) as r:
                for step in range(U + 4):
                    if step < U:
                        width = units[step][3]
                        act.wait_ge(maxed.sem, r * U + maxed.done(step))
                        act.wait_ge(turned.sem, r * U + turned.free(step))
                        act.activation(prob[:, step % R, 0:width], psS[:, step % R, 0:width], ACT.Exp,
                                       bias=nb[:, step % 4:step % 4 + 1], scale=SCALE,
                                       accum_out=sm[:, step % 4:step % 4 + 1]).then_inc(expd.sem, 1)
                    u = step - 2
                    if 0 <= u < U:
                        width = units[u][3]
                        w = min(width, P)
                        act.wait_ge(turned.sem, r * U + turned.done(u))
                        act.wait_ge(summed.sem, r * U + summed.free(u))
                        act.activation(probT[0:w, u % R, 0:max(width, P)], psT[0:w, u % R, 0:max(width, P)],
                                       ACT.Copy).then_inc(stored.sem, 1)
                    u = step - 4
                    if 0 <= u < U and u % per_tile == per_tile - 1:
                        t = units[u][1]
                        act.wait_ge(summed.sem, r * U + summed.done(u))
                        act.activation(o_out(r, t), psO[:, t % 2, 0:P], ACT.Copy).then_inc(out_done.sem, 1)
    copied.passed(copied_per * rounds)
    for s in (scored, maxed, expd, scaled, turned, stored, summed):
        s.passed(U * rounds)
    out_done.passed(TT * rounds)


def memory_attention(k, l, qm, mixT):
    with ExitStack() as c:
        kT = k.sb(c, f"ma_kT{l}", [P, MEM_CH, MEMLEN])
        v = k.sb(c, f"ma_v{l}", [P, MT, 2 * P])
        with ExitStack() as c2:
            mem = k.sb(c2, f"ma_mem{l}", [P, MT, D])
            memT = k.sb(c2, f"ma_memT{l}", [P, DC, MEMLEN])
            load(k, "mem", [(mem[:], k.dram["mem"].rearrange("(t p) d -> p t d", p=P))])
            norm_transpose(k, f"ma_n{l}", mem, MT, k.col(f"norm_mem{l}"), memT)
            project(k, f"ma_k{l}", k.dram[f"w_mem_k{l}"], MEM_CH, memT[:], MEMLEN, kT)
            natural(k, f"ma_vp{l}", k.dram[f"w_mem_v{l}"], 2 * P, memT, MT, v)
        head_norm(k, f"ma_kn{l}", kT[:], MEM_CH, MEMLEN, [k.col(f"mk_gain{l}")] * MEM_CH)
        head_norm(k, f"ma_qn{l}", qm, MEM_CH, S, [k.col(f"mq_gain{l}")] * MEM_CH)
        q_now = k.sb(c, f"ma_qs{l}", [P, S])
        k_now = k.sb(c, f"ma_ks{l}", [P, MEMLEN])
        v_now = k.sb(c, f"ma_vs{l}", [P, MT, P])
        units = [(half, t, k_now, MEMLEN, None, None, (lambda j, half=half: v_now[:, j, half * HD:(half + 1) * HD]))
                 for t in range(TT) for half in range(2)]
        staged = [
            (q_now[:], lambda r: qm[:, bass.ds(r, 1), :].rearrange("p a n -> p (a n)")),
            (k_now[:], lambda r: kT[:, bass.ds(r, 1), :].rearrange("p a n -> p (a n)")),
            (v_now[:], lambda r: v[:, :, bass.ds(r * P, P)]),
        ]
        attention(k, f"ma_at{l}", MEM_CH, staged, units,
                  lambda r, t: mixT[:, bass.ds(r + LRU_CH, 1), t * P:(t + 1) * P].rearrange("p a n -> p (a n)"))


def out_project(k, l, mixT, x):
    nc = k.nc
    loaded, product, added = k.sig("op_loaded"), k.sig("op_product"), k.sig("op_added", 4)
    with ExitStack() as c:
        w = k.sb(c, f"op_w{l}", [P, DC, D])
        ps = k.ps(c, f"op_ps{l}", [P, 4, 512])
        block = c.enter_context(nc.Block())

        @block.sync
        def _(sp):
            sp.dma_start(w[:], k.dram[f"w_out{l}"].rearrange("(c p) d -> p c d", p=P)).then_inc(loaded.sem, 16)

        @block.tensor
        def _(pe):
            pe.wait_ge(loaded.sem, loaded.base + 16)
            for n in range(2 * TT):
                t, h = n // 2, n % 2
                pe.wait_ge(added.sem, added.free(n))
                for dc in range(DC):
                    last = pe.matmul(ps[:, n % 4, :], mixT[:, dc, t * P:(t + 1) * P], w[:, dc, h * 512:(h + 1) * 512],
                                     start=(dc == 0), stop=(dc == DC - 1))
                last.then_inc(product.sem, 1)

        @block.vector
        def _(dve):
            added.give(dve)
            for n in range(2 * TT):
                t, h = n // 2, n % 2
                dve.wait_ge(product.sem, product.done(n))
                part = x[:, t, h * 512:(h + 1) * 512]
                dve.tensor_tensor(part, part, ps[:, n % 4, :], ALU.add).then_inc(added.sem, 1)
    loaded.passed(16)
    product.passed(2 * TT)
    added.passed(2 * TT)


def compress(k, tok, cos, sin, kc, vc):
    nc = k.nc
    loaded, blocked, hidden, acted, outd = (k.sig(x) for x in ("cp_loaded", "cp_blocked", "cp_hidden", "cp_acted", "cp_out"))
    LP = CMP_LEN // 2
    with ExitStack() as c:
        w1 = k.sb(c, "cp_w1", [P, 2, LP, HID])
        w2 = k.sb(c, "cp_w2", [P, 2, 2, HD])
        blk = k.sb(c, "cp_blk", [P, 2, LP, 2, CMPW])
        hid = k.sb(c, "cp_hid", [P, 2, 2, 2 * CMPW])
        ps = k.ps(c, "cp_ps", [P, 4, 512])
        psk = k.ps(c, "cp_psk", [P, 512])
        psv = k.ps(c, "cp_psv", [P, 512])
        with nc.Block() as block:
            @block.sync
            def _(sp):
                for j in range(2):
                    sp.dma_start(w1[:, j, :, :], k.dram["cmp_w1"][j].rearrange("(c p) h -> p c h", p=P)).then_inc(loaded.sem, 16)
                    sp.dma_start(w2[:, j, :, :], k.dram["cmp_w2"][j].rearrange("(c p) h -> p c h", p=P)).then_inc(loaded.sem, 16)

            @block.vector
            def _(dve):
                dve.memset(blk[:], 0.0)
                dve.drain()
                for j in range(2):
                    for g in range(2):
                        for l2 in range(2):
                            rows = slice(l2 * HD, (l2 + 1) * HD)
                            by_step = tok[rows, 2 * j + g, :].rearrange("p (n s) -> p s n", s=CMP_STRIDE)
                            for hi in range(2):
                                pos = k.col("cmp_pos", LP * j + 8 * hi, 8)[rows, :]
                                last = dve.tensor_tensor(blk[rows, j, 8 * hi:8 * hi + 8, g, 0:N_CMP],
                                                         by_step[:, l2::2, hi:hi + N_CMP],
                                                         bc(pos.unsqueeze(2), [HD, 8, N_CMP]), ALU.add)
                dve.drain()
                dve.memset(kc[:], 0.0).then_inc(blocked.sem, 1)

            @block.tensor
            def _(pe):
                pe.wait_ge(loaded.sem, loaded.base + 64)
                pe.wait_ge(blocked.sem, blocked.done(0))
                for j in range(2):
                    for h in range(2):
                        for lp in range(LP):
                            last = pe.matmul(ps[:, 2 * j + h, 0:2 * CMPW], w1[:, j, lp, h * P:(h + 1) * P],
                                             blk[:, j, lp, :, :], start=(lp == 0), stop=(lp == LP - 1))
                        last.then_inc(hidden.sem, 1)
                pe.wait_ge(acted.sem, acted.done(3))
                for g in range(2):
                    for h in range(2):
                        last = pe.matmul(psk[g * HD:(g + 1) * HD, 0:CMPW], w2[:, 0, h, :],
                                         hid[:, 0, h, g * CMPW:(g + 1) * CMPW], start=(h == 0), stop=(h == 1))
                last.then_inc(outd.sem, 1)
                for g in range(2):
                    for h in range(2):
                        last = pe.matmul(psv[0:CMPW, g * HD:(g + 1) * HD], hid[:, 1, h, g * CMPW:(g + 1) * CMPW],
                                         w2[:, 1, h, :], start=(h == 0), stop=(h == 1))
                last.then_inc(outd.sem, 1)

            @block.scalar
            def _(act):
                for n in range(4):
                    act.wait_ge(hidden.sem, hidden.done(n))
                    act.activation(hid[:, n // 2, n % 2, :], ps[:, n, 0:2 * CMPW], ACT.Gelu_apprx_tanh,
                                   bias=k.col("cmp_b1", n, 1)).then_inc(acted.sem, 1)
                act.wait_ge(outd.sem, outd.done(1))
                act.activation(kc[:, 0, 0:N_CMP], psk[:, 0:N_CMP], ACT.Copy)
                act.activation(vc[0:CMPW, :], psv[0:CMPW, 0:2 * HD], ACT.Copy)
    loaded.passed(64)
    blocked.passed(1)
    hidden.passed(4)
    acted.passed(4)
    outd.passed(2)
    at_block_end = lambda table: table[:].rearrange("p (n s) -> p n s", s=CMP_STRIDE)[:, 1:N_CMP + 1, CMP_STRIDE - 1]
    head_norm(k, "cp_hn", kc[:, :, 0:N_CMP], 1, N_CMP, [k.col("k_gain", 0, 1)], [(at_block_end(cos), at_block_end(sin))])


def nsa_gates(k, gates):
    nc = k.nc
    biased, opened = k.sig("ng_biased"), k.sig("ng_opened")
    with nc.Block() as block:
        @block.vector
        def _(dve):
            dve.tensor_tensor(gates[:], gates[:], bc(k.col("nsa_gate_b").unsqueeze(1), [P, TT, 36]), ALU.add).then_inc(biased.sem, 1)
            dve.wait_ge(opened.sem, opened.done(0))
            cmp0 = gates[:, 0, :].rearrange("p (h b) -> p h b", b=3)[:, :, 0]
            dve.tensor_scalar(cmp0, cmp0, k.col("rowvalid"), None, ALU.mult)

        @block.scalar
        def _(act):
            act.wait_ge(biased.sem, biased.done(0))
            act.activation(gates[:], gates[:], ACT.Sigmoid).then_inc(opened.sem, 1)
    biased.passed(1)
    opened.passed(1)


class UProducts:

    def __init__(self, k, c, l):
        self.k, self.l = k, l
        self.hhi = k.sb(c, f"up_hhi{l}", [P, DC, S], F32R)
        self.hlo = k.sb(c, f"up_hlo{l}", [P, DC, S], F32R)
        self.raw = k.sb(c, f"up_raw{l}", [P, GT, DC, P])
        self.hi = k.sb(c, f"up_hi{l}", [P, GT, DC, P], F32R)
        self.lo = k.sb(c, f"up_lo{l}", [P, GT, DC, P], F32R)
        self.z = k.sb(c, f"up_z{l}", [P, GT, S])
        self.ps = k.ps(c, f"up_ps{l}", [P, GT, 512])
        self.loaded = [k.sig("up_load0"), k.sig("up_load1")]
        self.hi_ready, self.lo_ready = k.sig("up_hi"), k.sig("up_lo", GT)
        self.dots, self.gelued = k.sig("up_dots", GT), k.sig("up_gelu", GT)
        self.kept, self.z_free = k.sig("up_kept"), k.sig("up_zfree", GT)

    def split_h(self, hT):
        nc, k = self.k.nc, self.k
        high = k.sig("up_hhigh")
        with nc.Block() as block:
            @block.scalar
            def _(act):
                act.activation(self.hhi[:], hT[:], ACT.Copy).then_inc(high.sem, 1)

            @block.vector
            def _(dve):
                dve.wait_ge(high.sem, high.done(0))
                dve.tensor_tensor(self.hlo[:], hT[:], self.hhi[:].bitcast(F32), ALU.subtract)
        high.passed(1)

    def load(self, sp, tile, a):
        sp.wait_ge(self.lo_ready.sem, tile + self.lo_ready.free(0))
        sp.dma_start(self.raw[:, a, :, :].unsqueeze(1), self.k.dram[f"uT{self.l}"][bass.ds(tile, 1), :, :, :].rearrange(
            "a p c e -> p a c e")).then_inc(self.loaded[a].sem, 16)

    def high(self, act, tile, a):
        act.wait_ge(self.loaded[a].sem, tile * 8 + (self.loaded[a].base + 16 - 8 * a))
        act.wait_ge(self.dots.sem, tile + self.dots.free(0))
        act.activation(self.hi[:, a, :, :], self.raw[:, a, :, :], ACT.Copy).then_inc(self.hi_ready.sem, 1)

    def low(self, dve, tile, a):
        dve.wait_ge(self.hi_ready.sem, tile + self.hi_ready.done(0))
        dve.tensor_tensor(self.lo[:, a, :, :], self.raw[:, a, :, :], self.hi[:, a, :, :].bitcast(F32),
                          ALU.subtract).then_inc(self.lo_ready.sem, 1)

    def product(self, pe, tile, a):
        pe.wait_ge(self.lo_ready.sem, tile + self.lo_ready.done(0))
        pe.wait_ge(self.gelued.sem, tile + self.gelued.free(0))
        for dc in range(DC):
            for m, (w, h) in enumerate(((self.hi, self.hhi), (self.hi, self.hlo), (self.lo, self.hhi))):
                last = pe.matmul(self.ps[:, a, :], w[:, a, dc, :], h[:, dc, :], start=(dc == 0 and m == 0),
                                 stop=(dc == DC - 1 and m == 2))
        last.then_inc(self.dots.sem, 1)

    def gelu(self, act, tile, a, free):
        act.wait_ge(self.dots.sem, tile + self.dots.done(0))
        free(tile)
        act.activation(self.z[:, a, :], self.ps[:, a, :], ACT.Gelu_apprx_tanh).then_inc(self.gelued.sem, 1)

    def early_gelu(self, act, tile, a):
        self.gelu(act, tile, a, lambda tile: act.wait_ge(self.z_free.sem, tile + self.z_free.free(0)))

    def keep(self, pool, zmat, tile, a):
        pool.wait_ge(self.gelued.sem, tile + self.gelued.done(0))
        pool.dma_start(zmat[:, bass.ds(tile, 1), :].rearrange("p a t -> p (a t)"), self.z[:, a, :]).then_inc(self.kept.sem, 16)
        pool.wait_ge(self.kept.sem, tile * 16 + self.kept.base + 16)
        pool.sem_inc(self.z_free.sem, 1)

    def finished(self):
        for s in self.loaded:
            s.passed(16 * NK // GT)
        for s in (self.hi_ready, self.lo_ready, self.dots, self.gelued):
            s.passed(NK)
        self.kept.passed(16 * EARLY)
        self.z_free.passed(EARLY)


def route(k, l, hT, up, zmat, valsb, key1, key2):
    nc = k.nc
    wq_loaded = [k.sig("ro_wq0"), k.sig("ro_wq1")]
    sk_loaded = [k.sig("ro_sk0"), k.sig("ro_sk1")]
    queried, q_stored, scored, s_stored = k.sig("ro_queried", 2), k.sig("ro_qstored", 2), k.sig("ro_scored", 2), k.sig("ro_sstored", 2)
    selected = k.sig("ro_selected", 1)
    with ExitStack() as c:
        wq = k.sb(c, f"ro_wq{l}", [P, 2, DC, P])
        sk = k.sb(c, f"ro_sk{l}", [P, 2, NK])
        q = k.sb(c, f"ro_q{l}", [P, 2, S])
        sc = k.sb(c, f"ro_s{l}", [P, 2, TT, NK])
        sc2 = k.sb(c, f"ro_s2{l}", [P, 2, TT, NK])
        top = k.sb(c, f"ro_top{l}", [P, 2, TT, TOPK])
        idx = k.sb(c, f"ro_idx{l}", [P, 2, TT, TOPK], U32)
        idxf = k.sb(c, f"ro_idxf{l}", [P, 2, TT, TOPK])
        cand = k.sb(c, f"ro_cand{l}", [P, TT, TOPK, TOPK])
        cand2 = k.sb(c, f"ro_cand2{l}", [P, TT, TOPK * TOPK])
        best = k.sb(c, f"ro_best{l}", [P, TT, TOPK])
        ci = k.sb(c, f"ro_ci{l}", [P, TT, TOPK], U32)
        pick = k.sb(c, f"ro_pick{l}", [P, 2, TT, TOPK], U32)
        pickf = k.sb(c, f"ro_pickf{l}", [P, 2, TT, TOPK])
        hot = k.sb(c, f"ro_hot{l}", [P, TT * TOPK, TOPK])
        keys = k.sb(c, f"ro_keys{l}", [P, 2, TT, TOPK])
        psq = k.ps(c, f"ro_psq{l}", [P, 2, 512])
        pss = k.ps(c, f"ro_pss{l}", [P, 2, TT, P])
        block = c.enter_context(nc.Block())
        w, subkeys = k.dram[f"peer_wq{l}"], k.dram[f"subkeys{l}"]

        @block.sync
        def _(sp):
            up.lo_ready.give(sp)
            for a in range(GT):
                up.load(sp, a, a)
            with sp.Fori(0, PH) as h:
                for b in range(2):
                    sp.wait_ge(queried.sem, h * 2 + queried.free(b))
                    sp.dma_start(wq[:, b, :, :], w[bass.ds(h * 2 + b, 1), :, :, :].rearrange("a p c m -> p (a c) m")
                                 ).then_inc(wq_loaded[b].sem, 16)
                    sp.wait_ge(scored.sem, h * 2 + scored.free(b))
                    sp.dma_start(sk[:, b, :], subkeys[bass.ds(h * 2 + b, 1), :, :].rearrange("a p n -> p (a n)")
                                 ).then_inc(sk_loaded[b].sem, 16)
                for a in range(GT):
                    up.load(sp, h * GT + (GT + a), a)

        @block.gpsimd
        def _(pool):
            up.z_free.give(pool)
            with pool.Fori(0, PH) as h:
                for a in range(GT):
                    up.keep(pool, zmat, h * GT + a, a)

        @block.tensor
        def _(pe):
            queried.give(pe)
            scored.give(pe)
            up.dots.give(pe)
            with pe.Fori(0, PH) as h:
                for b in range(2):
                    pe.wait_ge(wq_loaded[b].sem, h * 16 + wq_loaded[b].base + 16)
                    pe.wait_ge(q_stored.sem, h * 2 + q_stored.free(b))
                    for dc in range(DC):
                        last = pe.matmul(psq[:, b, :], wq[:, b, dc, :], hT[:, dc, :], start=(dc == 0), stop=(dc == DC - 1))
                    last.then_inc(queried.sem, 1)
                up.product(pe, h * GT, 0)
                for b in range(2):
                    pe.wait_ge(sk_loaded[b].sem, h * 16 + sk_loaded[b].base + 16)
                    pe.wait_ge(q_stored.sem, h * 2 + q_stored.done(b))
                    pe.wait_ge(s_stored.sem, h * 2 + s_stored.free(b))
                    for t in range(TT):
                        last = pe.matmul(pss[:, b, t, :], q[:, b, t * P:(t + 1) * P], sk[:, b, :], start=True, stop=True)
                    last.then_inc(scored.sem, 1)
                up.product(pe, h * GT + 1, 1)

        @block.scalar
        def _(act):
            q_stored.give(act)
            s_stored.give(act)
            up.gelued.give(act)
            up.high(act, 0, 0)
            with act.Fori(0, PH) as h:
                up.high(act, h * GT + 1, 1)
                for b in range(2):
                    act.wait_ge(queried.sem, h * 2 + queried.done(b))
                    act.wait_ge(scored.sem, h * 2 + scored.free(b))
                    act.activation(q[:, b, :], psq[:, b, :], ACT.Copy).then_inc(q_stored.sem, 1)
                up.early_gelu(act, h * GT, 0)
                up.high(act, h * GT + GT, 0)
                act.wait_ge(selected.sem, h + selected.free(0))
                for b in range(2):
                    act.wait_ge(scored.sem, h * 2 + scored.done(b))
                    act.activation(sc[:, b, :, :], pss[:, b, :, :], ACT.Copy).then_inc(s_stored.sem, 1)
                up.early_gelu(act, h * GT + 1, 1)

        @block.vector
        def _(dve):
            selected.give(dve)
            up.low(dve, 0, 0)
            with dve.Fori(0, PH) as h:
                up.low(dve, h * GT + 1, 1)
                up.low(dve, h * GT + GT, 0)
                dve.wait_ge(s_stored.sem, h * 2 + s_stored.done(1))
                dve.memset(hot[:, 0, 0:1], 0.0)
                pairs = [(b, t) for b in range(2) for t in range(TT)]
                for b, t in pairs:
                    dve.max(top[:, b, t, 0:8], sc[:, b, t, :])
                dve.drain()
                for b, t in pairs:
                    dve.max_index(idx[:, b, t, 0:8], top[:, b, t, 0:8], sc[:, b, t, :])
                    dve.match_replace(sc2[:, b, t, :], top[:, b, t, 0:8], sc[:, b, t, :], -3.0e38)
                dve.drain()
                for b, t in pairs:
                    dve.max(top[:, b, t, 8:16], sc2[:, b, t, :])
                dve.drain()
                for b, t in pairs:
                    dve.max_index(idx[:, b, t, 8:16], top[:, b, t, 8:16], sc2[:, b, t, :])
                dve.drain()
                dve.tensor_copy(idxf[:], idx[:])
                for t in range(TT):
                    dve.tensor_tensor(cand[:, t, :, :], bc(top[:, 0, t, :].unsqueeze(2), [P, TOPK, TOPK]),
                                      bc(top[:, 1, t, :].unsqueeze(1), [P, TOPK, TOPK]), ALU.add)
                dve.drain()
                flat = cand[:].rearrange("p t a b -> p t (a b)")
                for t in range(TT):
                    dve.max(best[:, t, 0:8], flat[:, t, :])
                dve.drain()
                for t in range(TT):
                    dve.max_index(ci[:, t, 0:8], best[:, t, 0:8], flat[:, t, :])
                    dve.match_replace(cand2[:, t, :], best[:, t, 0:8], flat[:, t, :], -3.0e38)
                dve.drain()
                for t in range(TT):
                    dve.max(best[:, t, 8:16], cand2[:, t, :])
                dve.drain()
                for t in range(TT):
                    dve.max_index(ci[:, t, 8:16], best[:, t, 8:16], cand2[:, t, :])
                dve.drain()
                dve.tensor_scalar(pick[:, 0, :, :], ci[:], 4, None, ALU.logical_shift_right)
                dve.tensor_scalar(pick[:, 1, :, :], ci[:], 15, None, ALU.bitwise_and)
                dve.drain()
                dve.tensor_copy(pickf[:], pick[:])
                dve.drain()
                iota = bc(k.col("iota", 0, TOPK).unsqueeze(1), [P, TT * TOPK, TOPK])
                for b in range(2):
                    dve.tensor_tensor(hot[:], bc(pickf[:, b, :, :].rearrange("p t k -> p (t k)").unsqueeze(2),
                                                 [P, TT * TOPK, TOPK]), iota, ALU.is_equal)
                    dve.drain()
                    hot4 = hot[:].rearrange("p (t k) a -> p t k a", t=TT)
                    dve.tensor_tensor(hot4, hot4, bc(idxf[:, b, :, :].unsqueeze(2), [P, TT, TOPK, TOPK]), ALU.mult)
                    dve.drain()
                    dve.tensor_reduce(keys[:, b, :, :].rearrange("p t k -> p (t k)"), hot[:], AX.X, ALU.add)
                    dve.drain()
                at = bass.ds(h * TOPK, TOPK)
                dve.tensor_copy(key1[:, :, at], keys[:, 0, :, :])
                dve.tensor_copy(key2[:, :, at], keys[:, 1, :, :])
                dve.tensor_copy(valsb[:, :, at], best[:]).then_inc(selected.sem, 1)
                dve.drain()
    for s in (*wq_loaded, *sk_loaded):
        s.passed(16 * PH)
    for s in (queried, q_stored, scored, s_stored):
        s.passed(2 * PH)
    selected.passed(PH)


def gate_softmax(k, l, vals, key1, key2, rows):
    nc = k.nc
    shifted, expd, ready, turned = (k.sig(x) for x in ("gs_shifted", "gs_exp", "gs_ready", "gs_turned"))
    with ExitStack() as c:
        total = k.sb(c, f"gs_total{l}", [P, TT * PH])
        ps = k.ps(c, f"gs_ps{l}", [P, 3, TT, P])
        block = c.enter_context(nc.Block())
        by_head = vals[:].rearrange("p t (h k) -> p (t h) k", k=TOPK)
        n = TT * PH

        @block.vector
        def _(dve):
            dve.tensor_copy(total[:].unsqueeze(2), by_head[:, :, 0:1])
            dve.drain()
            dve.tensor_tensor(by_head, by_head, bc(total[:].unsqueeze(2), [P, n, TOPK]), ALU.subtract).then_inc(shifted.sem, 1)
            dve.wait_ge(expd.sem, expd.done(0))
            dve.tensor_reduce(total[:], by_head, AX.X, ALU.add)
            dve.drain()
            dve.reciprocal(total[:], total[:])
            dve.drain()
            dve.tensor_tensor(by_head, by_head, bc(total[:].unsqueeze(2), [P, n, TOPK]), ALU.mult).then_inc(ready.sem, 1)
            for j in range(3):
                dve.wait_ge(turned.sem, turned.done(j))
                dve.tensor_copy(rows[:, j, :], ps[:, j, :, :].rearrange("p t n -> p (t n)"))

        @block.scalar
        def _(act):
            act.wait_ge(shifted.sem, shifted.done(0))
            act.activation(vals[:], vals[:], ACT.Exp).then_inc(expd.sem, 1)

        @block.tensor
        def _(pe):
            pe.wait_ge(ready.sem, ready.done(0))
            for j, src in enumerate((key1, key2, vals)):
                for t in range(TT):
                    last = pe.transpose(ps[:, j, t, :], src[:, t, :], k.col("ident"))
                last.then_inc(turned.sem, 1)
    for s in (shifted, expd, ready):
        s.passed(1)
    turned.passed(3)


def spread_gates(k, l, rows, up, zmat, gmat):
    nc = k.nc
    staged, spread, stored, written = k.sig("sg_staged"), k.sig("sg_spread", 4), k.sig("sg_stored", 4), k.sig("sg_written")
    gbuf_free = k.sig("sg_gbuf", 2)
    Q = 4
    NQ = TB // Q
    T0 = GT * PH
    R = 4
    with ExitStack() as c:
        now = k.sb(c, f"sg_now{l}", [P, 3, TB])
        left = k.sb(c, f"sg_left{l}", [P, R, Q, NK])
        right = k.sb(c, f"sg_right{l}", [P, R, Q, NK])
        gbuf = k.sb(c, f"sg_gbuf{l}", [P, 2, NK, TB])
        ps = k.ps(c, f"sg_ps{l}", [P, R, Q, NK])
        block = c.enter_context(nc.Block())
        iota = k.col("iota")

        @block.vector
        def _(dve):
            with dve.Fori(0, NTB // 2) as i:
                for par in range(2):
                    blk = i * 2 + par
                    dve.drain()
                    dve.tensor_copy(now[:], rows[:, :, bass.ds(blk * TB, TB)])
                    dve.drain()
                    for n in range(NQ):
                        if n == 4:
                            up.low(dve, blk * GT + (T0 + 1), 1)
                        if n == 12:
                            up.low(dve, blk * GT + (T0 + GT), 0)
                        dve.wait_ge(spread.sem, blk * NQ + spread.free(n))
                        dve.tensor_tensor(left[:, n % R, :, :], bc(iota.unsqueeze(1), [P, Q, NK]),
                                          bc(now[:, 1, n * Q:(n + 1) * Q].unsqueeze(2), [P, Q, NK]), ALU.is_equal)
                        for j in range(Q):
                            t = n * Q + j
                            last = dve.tensor_scalar(right[:, n % R, j, :], iota, now[:, 0, t:t + 1], now[:, 2, t:t + 1],
                                                     ALU.is_equal, ALU.mult)
                        last.then_inc(staged.sem, 1)

        @block.tensor
        def _(pe):
            spread.give(pe)
            with pe.Fori(0, NTB // 2) as i:
                for par in range(2):
                    blk = i * 2 + par
                    for n in range(NQ):
                        pe.wait_ge(staged.sem, blk * NQ + staged.done(n))
                        pe.wait_ge(stored.sem, blk * NQ + stored.free(n))
                        for j in range(Q):
                            last = pe.matmul(ps[:, n % R, j, :], left[:, n % R, j, :], right[:, n % R, j, :], start=True, stop=True)
                        last.then_inc(spread.sem, 1)
                        if n == NQ // 2 - 1:
                            up.product(pe, blk * GT + T0, 0)
                    up.product(pe, blk * GT + (T0 + 1), 1)

        @block.scalar
        def _(act):
            stored.give(act)
            with act.Fori(0, NTB // 2) as i:
                for par in range(2):
                    blk = i * 2 + par
                    up.high(act, blk * GT + (T0 + 1), 1)
                    act.wait_ge(gbuf_free.sem, blk + gbuf_free.free(0))
                    for n in range(NQ):
                        act.wait_ge(spread.sem, blk * NQ + spread.done(n))
                        act.activation(gbuf[:, par, :, n * Q:(n + 1) * Q].rearrange("p i t -> p t i"), ps[:, n % R, :, :],
                                       ACT.Copy).then_inc(stored.sem, 1)
                        if n == NQ // 2 - 1:
                            up.early_gelu(act, blk * GT + T0, 0)
                            up.high(act, blk * GT + (T0 + GT), 0)
                    up.early_gelu(act, blk * GT + (T0 + 1), 1)

        @block.gpsimd
        def _(pool):
            with pool.Fori(0, NTB // 2) as i:
                for par in range(2):
                    blk = i * 2 + par
                    for a in range(GT):
                        up.keep(pool, zmat, blk * GT + (T0 + a), a)

        @block.sync
        def _(sp):
            gbuf_free.give(sp)
            with sp.Fori(0, NTB // 2) as i:
                for par in range(2):
                    blk = i * 2 + par
                    for a in range(GT):
                        up.load(sp, blk * GT + (T0 + GT + a), a)
                    sp.wait_ge(stored.sem, blk * NQ + stored.done(NQ - 1))
                    sp.dma_start(gmat[:, bass.ds(blk, 1), :, :].rearrange("p a i t -> p (a i t)"),
                                 gbuf[:, par, :, :].rearrange("p i t -> p (i t)")).then_inc(written.sem, 16)
                    sp.wait_ge(written.sem, blk * 16 + written.base + 16)
                    sp.sem_inc(gbuf_free.sem, 1)
    for s in (staged, spread, stored):
        s.passed(NTB * NQ)
    written.passed(16 * NTB)
    gbuf_free.passed(NTB)


def experts(k, l, up, x, zmat, gmat):
    nc = k.nc
    v_loaded = [k.sig("ex_vload0"), k.sig("ex_vload1")]
    g_loaded = [k.sig("ex_gload0"), k.sig("ex_gload1")]
    z_loaded = [k.sig("ex_zload0"), k.sig("ex_zload1")]
    v_hi, v_lo = k.sig("ex_vhi"), k.sig("ex_vlo", 2)
    weighted, ready = k.sig("ex_weighted", 2), k.sig("ex_ready", 2)
    summed, added = k.sig("ex_summed"), k.sig("ex_added", 4)
    NO = 2 * TT
    with ExitStack() as c:
        vr = k.sb(c, f"ex_vr{l}", [P, GT, D])
        vh = k.sb(c, f"ex_vh{l}", [P, 2, GT, D], F32R)
        vl = k.sb(c, f"ex_vl{l}", [P, 2, GT, D], F32R)
        gm = k.sb(c, f"ex_gm{l}", [P, 2, NTB, GT, TB])
        ah = k.sb(c, f"ex_ah{l}", [P, 2, GT, S], F32R)
        al = k.sb(c, f"ex_al{l}", [P, 2, GT, S], F32R)
        psy = k.ps(c, f"ex_psy{l}", [P, 4, 512])
        block = c.enter_context(nc.Block())
        v_d = k.dram[f"v{l}"]

        def nth(s, g, par, n=0):
            return g * 8 + (s.base + 16 - 8 * par)

        @block.sync
        def _(sp):
            def load_gates(g, par):
                sp.wait_ge(ready.sem, g + ready.free(0))
                sp.dma_start(gm[:, par, :, :, :].rearrange("p b i t -> p b (i t)"),
                             gmat[:, :, bass.ds(g * GT, GT), :].rearrange("p b i t -> p b (i t)")
                             ).then_inc(g_loaded[par].sem, 16)

            def load_v(g, a):
                sp.wait_ge(v_lo.sem, g * GT + v_lo.free(a))
                sp.dma_start(vr[:, a, :], v_d[bass.ds(g * (GT * P) + a * P, P), :]).then_inc(v_loaded[a].sem, 16)

            def load_z(g, a):
                sp.wait_ge(weighted.sem, g * GT + weighted.free(a))
                sp.dma_start(up.z[:, a, :], zmat[:, bass.ds(g * GT + a, 1), :].rearrange("p a t -> p (a t)")
                             ).then_inc(z_loaded[a].sem, 16)

            with sp.Fori(0, EG // 2) as i:
                for par in range(2):
                    g = i * 2 + par
                    load_gates(g, par)
                    for a in range(GT):
                        load_v(g, a)
                    for a in range(GT):
                        load_z(g, a)
            with sp.Fori(EG // 2, NG // 2 - 1) as i:
                for par in range(2):
                    g = i * 2 + par
                    load_gates(g, par)
                    for a in range(GT):
                        load_v(g, a)
                        up.load(sp, g * GT + (GT + a), a)
            for g in (NG - 2, NG - 1):
                load_gates(g, g % 2)
                for a in range(GT):
                    load_v(g, a)
                    if g < NG - 1:
                        up.load(sp, (g + 1) * GT + a, a)

        @block.tensor
        def _(pe):
            def u_products(g):
                for a in range(GT):
                    up.product(pe, g * GT + a, a)

            def v_products(g, par):
                pe.wait_ge(ready.sem, g + ready.done(0))
                for o in range(NO):
                    t, h = o // 2, o % 2
                    cols, toks = slice(h * 512, (h + 1) * 512), slice(t * P, (t + 1) * P)
                    pe.wait_ge(added.sem, g * NO + added.free(o))
                    for a in range(GT):
                        for m, (w, v) in enumerate(((ah, vh), (ah, vl), (al, vh))):
                            last = pe.matmul(psy[:, o % 4, :], w[:, par, a, toks], v[:, par, a, cols],
                                             start=(a == 0 and m == 0), stop=(a == GT - 1 and m == 2))
                    last.then_inc(summed.sem, 1)

            with pe.Fori(0, EG // 2 - 1) as i:
                v_products(i * 2, 0)
                v_products(i * 2 + 1, 1)
            v_products(EG - 2, 0)
            u_products(EG)
            v_products(EG - 1, 1)
            with pe.Fori(EG // 2, NG // 2 - 1) as i:
                u_products(i * 2 + 1)
                v_products(i * 2, 0)
                u_products(i * 2 + 2)
                v_products(i * 2 + 1, 1)
            u_products(NG - 1)
            v_products(NG - 2, 0)
            v_products(NG - 1, 1)

        @block.scalar
        def _(act):
            def v_high(g, par):
                for a in range(GT):
                    act.wait_ge(v_loaded[a].sem, g * 16 + v_loaded[a].base + 16)
                    act.activation(vh[:, par, a, :], vr[:, a, :], ACT.Copy).then_inc(v_hi.sem, 1)

            def half_free(g):
                act.wait_ge(summed.sem, g * NO + (summed.base - NO))

            def step(g, par, more=True):
                v_high(g, par)
                for a in range(GT):
                    up.gelu(act, g * GT + a, a, lambda tile: act.wait_ge(weighted.sem, tile + weighted.free(0)))
                    if more:
                        up.high(act, g * GT + (GT + a), a)

            v_high(0, 0)
            v_high(1, 1)
            with act.Fori(1, EG // 2) as i:
                for par in range(2):
                    half_free(i * 2 + par)
                    v_high(i * 2 + par, par)
            up.high(act, EARLY + 1, 1)
            with act.Fori(EG // 2, NG // 2 - 1) as i:
                for par in range(2):
                    half_free(i * 2 + par)
                    step(i * 2 + par, par)
            half_free(NG - 2)
            step(NG - 2, 0)
            half_free(NG - 1)
            step(NG - 1, 1, more=False)

        @block.vector
        def _(dve):
            v_lo.give(dve)
            weighted.give(dve)
            ready.give(dve)
            added.give(dve)

            def v_low(g, par):
                for a in range(GT):
                    dve.wait_ge(v_hi.sem, g * GT + v_hi.done(a))
                    dve.tensor_tensor(vl[:, par, a, :], vr[:, a, :], vh[:, par, a, :].bitcast(F32),
                                      ALU.subtract).then_inc(v_lo.sem, 1)

            def weigh(g, par, a, z_ready):
                if a == 0:
                    dve.wait_ge(g_loaded[par].sem, nth(g_loaded[par], g, par))
                z_ready(g, a)
                blocks = up.z[:, a, :].rearrange("p (b t) -> p b t", t=TB)
                dve.tensor_tensor(blocks, blocks, gm[:, par, :, a, :], ALU.mult)
                dve.drain()
                dve.tensor_copy(ah[:, par, a, :], up.z[:, a, :])
                dve.drain()
                dve.tensor_tensor(al[:, par, a, :], up.z[:, a, :], ah[:, par, a, :].bitcast(F32),
                                  ALU.subtract).then_inc(weighted.sem, 1)
                if a == GT - 1:
                    dve.wait_ge(weighted.sem, g * GT + weighted.done(a))
                    dve.sem_inc(ready.sem, 1)

            def add(g, outs):
                dve.drain()
                for o in outs:
                    t, h = o // 2, o % 2
                    dve.wait_ge(summed.sem, g * NO + summed.done(o))
                    part = x[:, t, h * 512:(h + 1) * 512]
                    dve.tensor_tensor(part, part, psy[:, o % 4, :], ALU.add).then_inc(added.sem, 1)

            from_dram = lambda g, a: dve.wait_ge(z_loaded[a].sem, g * 16 + z_loaded[a].base + 16)
            from_gelu = lambda g, a: dve.wait_ge(up.gelued.sem, g * GT + up.gelued.done(a))

            def early_step(g, par, adds=True):
                v_low(g, par)
                weigh(g, par, 0, from_dram)
                if adds:
                    add(g - 1, range(0, NO // 2))
                weigh(g, par, 1, from_dram)
                if adds:
                    add(g - 1, range(NO // 2, NO))

            def step(g, par, more=True):
                v_low(g, par)
                weigh(g, par, 0, from_gelu)
                if more:
                    up.low(dve, g * GT + GT, 0)
                weigh(g, par, 1, from_gelu)
                add(g - 1, range(0, NO // 2))
                if more:
                    up.low(dve, g * GT + (GT + 1), 1)
                add(g - 1, range(NO // 2, NO))

            early_step(0, 0, adds=False)
            early_step(1, 1)
            with dve.Fori(1, EG // 2) as i:
                early_step(i * 2, 0)
                early_step(i * 2 + 1, 1)
            up.low(dve, EARLY + 1, 1)
            with dve.Fori(EG // 2, NG // 2 - 1) as i:
                step(i * 2, 0)
                step(i * 2 + 1, 1)
            step(NG - 2, 0)
            step(NG - 1, 1, more=False)
            add(NG - 1, range(NO))
    up.finished()
    for s in v_loaded:
        s.passed(16 * NG)
    for s in g_loaded:
        s.passed(8 * NG)
    for s in z_loaded:
        s.passed(16 * EG)
    for s in (v_hi, v_lo, weighted):
        s.passed(NK)
    ready.passed(NG)
    summed.passed(NG * NO)
    added.passed(NG * NO)


def peer(k, l, x, zmat, gmat):
    with ExitStack() as c:
        up = UProducts(k, c, l)
        with ExitStack() as c2:
            vals = k.sb(c2, f"pe_vals{l}", [P, TT, HK])
            key1 = k.sb(c2, f"pe_key1{l}", [P, TT, HK])
            key2 = k.sb(c2, f"pe_key2{l}", [P, TT, HK])
            rows = k.sb(c2, f"pe_rows{l}", [P, 3, S])
            with ExitStack() as c3:
                hT = k.sb(c3, f"pe_hT{l}", [P, DC, S])
                norm_transpose(k, f"pe_n{l}", x, TT, k.col(f"norm_ffn{l}"), hT)
                up.split_h(hT)
                route(k, l, hT, up, zmat, vals, key1, key2)
            gate_softmax(k, l, vals, key1, key2, rows)
            spread_gates(k, l, rows, up, zmat, gmat)
        experts(k, l, up, x, zmat, gmat)


def build(nc, dram, out, stop=99):
    with ExitStack() as ctx:
        k = Chip(nc, ctx)
        k.dram = dram
        k.params = k.sb(ctx, "params_sb", [P, NCOLS])
        x = k.sb(ctx, "x_sb", [P, TT, D])
        gmat = nc.dram_tensor("gate_matrix", (P, NTB, NK, TB), F32, kind="Internal").ap()
        zmat = nc.dram_tensor("early_gelu", (P, EARLY, S), F32, kind="Internal").ap()
        load(k, "params", [(k.params[:], dram["params"]), (x[:], dram["x"].rearrange("(t p) d -> p t d", p=P))])

        def finish():
            stored = k.sig("out_stored")
            with nc.Block() as block:
                @block.sync
                def _(sp):
                    sp.dma_start(out.rearrange("(t p) d -> p t d", p=P), x[:]).then_inc(stored.sem, 16)
                    sp.wait_ge(stored.sem, stored.base + 16)

        with ExitStack() as c:
            mixT = k.sb(c, "mixT0", [P, DC, S])
            proj = k.sb(c, "proj0", [P, 2 * LRU_CH + MEM_CH, S])
            with ExitStack() as c2:
                hT = k.sb(c2, "hT0", [P, DC, S])
                norm_transpose(k, "n0", x, TT, k.col("norm_mix0"), hT)
                project(k, "p0", dram["a_w_in"], 2 * LRU_CH + MEM_CH, hT[:], S, proj)
            recurrent(k, proj, mixT)
            memory_attention(k, 0, proj[:, 2 * LRU_CH:, :], mixT)
            out_project(k, 0, mixT, x)
        if stop >= 2:
            peer(k, 0, x, zmat, gmat)
        if stop >= 3:
            with ExitStack() as c:
                cos = k.sb(c, "rope_cos", [P, S])
                sin = k.sb(c, "rope_sin", [P, S])
                rope_tables(k, cos, sin)
                kc = k.sb(c, "kc", [P, 1, CMPW])
                vc = k.sb(c, "vc", [CMPW, 2 * HD])
                keysT = k.sb(c, "keysT", [P, 6, S])
                vals = k.sb(c, "vals", [P, TT, 4 * HD])
                with ExitStack() as c2:
                    hT = k.sb(c2, "hTkv", [P, DC, S])
                    norm_transpose(k, "nkv", x, TT, k.col("kv_norm"), hT)
                    project(k, "pkv", dram["w_keys"], 6, hT[:], S, keysT)
                    natural(k, "pv", dram["w_vals"], 4 * HD, hT, TT, vals)
                head_norm(k, "hk", keysT[:, 4:6, :], 2, S, [k.col("k_gain", 1, 1), k.col("k_gain", 2, 1)],
                          [(cos[:], sin[:])] * 2)
                compress(k, keysT, cos, sin, kc, vc)
                mixT = k.sb(c, "mixT1", [P, DC, S])
                proj = k.sb(c, "proj1", [P, DC, S])
                gates = k.sb(c, "gates", [P, TT, 36])
                with ExitStack() as c2:
                    hT = k.sb(c2, "hT1", [P, DC, S])
                    norm_transpose(k, "n1", x, TT, k.col("norm_mix1"), hT)
                    project(k, "p1", dram["b_w_in"], DC, hT[:], S, proj)
                    natural(k, "pg", dram["w_gates"], 36, hT, TT, gates)
                nsa_gates(k, gates)
                head_norm(k, "hq", proj[:, 0:LRU_CH, :], LRU_CH, S, [k.col("q_gain")] * LRU_CH, [(cos[:], sin[:])] * LRU_CH)
                with ExitStack() as c2:
                    q_now = k.sb(c2, "q_now", [P, S])
                    gate_now = k.sb(c2, "gate_now", [P, TT, 6])
                    units = []
                    for t in range(TT):
                        for half in range(2):
                            gate = lambda b: gate_now[:, t, 3 * half + b:3 * half + b + 1]
                            cols = slice(half * HD, (half + 1) * HD)
                            units.append((half, t, kc[:, 0, :], CMPW, k.col("cmpmask", t * CMPW, CMPW), gate(0),
                                          (lambda j, cols=cols: vc[:, cols])))
                            for b in range(2):
                                at = slice(2 * b * HD + half * HD, 2 * b * HD + (half + 1) * HD)
                                units.append((half, t, keysT[:, 4 + b, :], (t + 1) * P, k.col("causal"), gate(1 + b),
                                              (lambda j, at=at: vals[:, j, at])))
                    staged = [
                        (q_now[:], lambda r: proj[:, bass.ds(r, 1), :].rearrange("p a n -> p (a n)")),
                        (gate_now[:], lambda r: gates[:, :, bass.ds(r * 6, 6)]),
                    ]
                    attention(k, "nsa", LRU_CH, staged, units,
                              lambda r, t: mixT[:, bass.ds(r, 1), t * P:(t + 1) * P].rearrange("p a n -> p (a n)"))
                memory_attention(k, 1, proj[:, LRU_CH:, :], mixT)
                out_project(k, 1, mixT, x)
        if stop >= 4:
            peer(k, 1, x, zmat, gmat)
        finish()


def chunks_T(w):
    return np.ascontiguousarray(w.reshape(DC, P, -1, P).transpose(2, 1, 0, 3))


def rows_first(w):
    return np.ascontiguousarray(w.reshape(DC, P, -1).transpose(1, 0, 2))


def shape_constants():
    rot = np.zeros((P, P), np.float32)
    mean = np.zeros((P, P), np.float32)
    for h in (0, HD):
        mean[h:h + HD, h:h + HD] = 1.0 / HD
        for i in range(ROPE_HALF):
            rot[h + ROPE_HALF + i, h + i] = -1.0
            rot[h + i, h + ROPE_HALF + i] = 1.0
    freq = np.zeros((P, 1), np.float32)
    f = np.float32(THETA) ** (-np.arange(ROPE_HALF, dtype=np.float32) / np.float32(ROPE_HALF))
    for h in (0, HD):
        freq[h:h + ROPE_HALF, 0] = f
        freq[h + ROPE_HALF:h + 2 * ROPE_HALF, 0] = f
    t = np.arange(P)
    causal = np.where(t[None, :] <= t[:, None], 0.0, NEG).astype(np.float32)
    end = np.arange(CMPW) * CMP_STRIDE + CMP_LEN - 1
    tok = np.arange(S).reshape(TT, P)
    cmp = np.where((end[None, None] <= tok[:, :, None]) & (np.arange(CMPW) < N_CMP)[None, None], 0.0, NEG)
    return {
        "ident": np.eye(P, dtype=np.float32), "rot": rot, "headmean": mean, "causal": causal,
        "cmpmask": cmp.transpose(1, 0, 2).reshape(P, TT * CMPW).astype(np.float32),
        "iota": np.tile(np.arange(P, dtype=np.float32), (P, 1)), "freq": freq,
        "rowvalid": (t >= CMP_LEN - 1).astype(np.float32)[:, None],
    }


def laid_out(i):
    by_channel = lambda v: v.reshape(-1, P).T
    twice = lambda v: np.concatenate([v, v])[:, None]
    cols = shape_constants()
    for l in range(LAYERS):
        cols[f"norm_mix{l}"] = by_channel(i["norm_mix"][l])
        cols[f"norm_ffn{l}"] = by_channel(i["norm_ffn"][l])
        cols[f"norm_mem{l}"] = by_channel(i["norm_mem"][l])
        cols[f"mq_gain{l}"] = twice(i["mem_q_gain"][l])
        cols[f"mk_gain{l}"] = twice(i["mem_k_gain"][l])
    cols["kv_norm"] = by_channel(i["kv_norm"])
    cols["conv_w"] = i["a_conv_w"][0].T.reshape(LRU_CH, P, 4).transpose(1, 0, 2).reshape(P, -1)
    cols["conv_b"] = by_channel(i["a_conv_b"][0])
    cols["gate_b"] = np.concatenate([by_channel(i["a_gate_b"][0, g]) for g in range(2)], axis=1)
    cols["lam"] = by_channel(i["a_lambda"][0])
    cols["q_gain"] = twice(i["b_q_gain"][0])
    cols["k_gain"] = np.concatenate([twice(i["k_gain_shared"][b]) for b in range(3)], axis=1)
    cols["cmp_b1"] = np.concatenate([by_channel(i["cmp_b1"][j]) for j in range(2)], axis=1)
    heads = [h for c in range(LRU_CH) for h in (c, c + LRU_CH)]
    cols["nsa_gate_b"] = np.tile(i["b_gate_b"][0].reshape(12, 3)[heads].reshape(1, 36), (P, 1))
    cols["cmp_pos"] = i["cmp_pos"].reshape(2, CMP_LEN // 2, 2, HD).transpose(2, 3, 0, 1).reshape(P, -1)
    a = {"params": np.ascontiguousarray(np.concatenate([cols[n].reshape(P, w) for n, w in COLS], axis=1))}
    a["x"], a["mem"], a["positions"] = i["x"][0], i["mem"][0], i["positions"]
    a["a_w_in"] = chunks_T(i["a_w_in"][0])
    gw = np.zeros((P, LRU_CH, 2, P), np.float32)
    for c in range(LRU_CH):
        for g in range(2):
            for h in range(2):
                gw[h * HD:(h + 1) * HD, c, g, h * HD:(h + 1) * HD] = i["a_gate_w"][0, g, 2 * c + h]
    a["gate_w"] = gw
    w = i["b_w_in"][0]
    q = w[:, :768].reshape(D, 12, HD)[:, heads].reshape(D, 768)
    a["b_w_in"] = chunks_T(np.concatenate([q, w[:, 804:]], axis=1))
    a["w_gates"] = rows_first(w[:, 768:804].reshape(D, 12, 3)[:, heads].reshape(D, 36))
    kv = i["w_kv_shared"].reshape(D, 3, 2, 2, HD)
    dup = lambda m: np.concatenate([m, m], axis=1)
    a["w_keys"] = chunks_T(np.concatenate(
        [dup(kv[:, 0, j, g]) for j in range(2) for g in range(2)] + [kv[:, b, 0].reshape(D, P) for b in (1, 2)], axis=1))
    a["w_vals"] = rows_first(np.concatenate([kv[:, b, 1].reshape(D, P) for b in (1, 2)], axis=1))
    a["cmp_w1"], a["cmp_w2"] = i["cmp_w1"], i["cmp_w2"]
    for l in range(LAYERS):
        a[f"w_mem_k{l}"] = chunks_T(i["w_mem_kv"][l][:, :256])
        a[f"w_mem_v{l}"] = rows_first(i["w_mem_kv"][l][:, 256:])
        w = i["w_out"][l]
        if l:
            w = np.concatenate([w[:768].reshape(12, HD, D)[heads].reshape(768, D), w[768:]], axis=0)
        a[f"w_out{l}"] = w
        a[f"peer_wq{l}"] = chunks_T(i["peer_wq"][l])
        a[f"subkeys{l}"] = i["peer_subkeys"][l].reshape(2 * PH, NK, P).transpose(0, 2, 1)
        a[f"uT{l}"] = i["peer_u"][l].reshape(NK, P, DC, P).transpose(0, 3, 2, 1)
        a[f"v{l}"] = i["peer_v"][l]
    return {n: np.ascontiguousarray(v) for n, v in a.items()}


STOP = 99


def kernel(**inputs):
    import concourse.bacc as bacc
    from concourse.bass_utils import run_bass_kernel_spmd as run

    nc = bacc.Bacc("TRN2", target_bir_lowering=False, num_devices=1)
    arrays = laid_out({n: np.asarray(v) for n, v in inputs.items()})
    dram = {n: nc.dram_tensor("in_" + n, v.shape, mybir.dt.from_np(v.dtype), kind="ExternalInput").ap()
            for n, v in arrays.items()}
    out = nc.dram_tensor("out", (S, D), F32, kind="ExternalOutput").ap()
    build(nc, dram, out, STOP)
    r = run(nc, [{"in_" + n: v for n, v in arrays.items()}], core_ids=[0])
    return r.results[0]["out"][None]
```
